# Optimizing a Trainium2 kernel written in Bass

```python
import math
import jax, jax.numpy as jnp
from jax import lax
import numpy as np

D_MODEL = 1024
BATCH = 1
SEQ = 256
DEPTH = 2

CTX_LEN = 256
GRID_W = 64
HEAD_DIM = 64
D_CONV = 256
CONV_W = 3
H_NA = 6
WIN_R_MAX = 8
WIN_C = 16
H_Q = 6
H_KV = 2
WINDOW = 128
BLK_Q = 128
ROPE_BASE = 10000.0
D_NA = H_NA * HEAD_DIM
D_SW = H_Q * HEAD_DIM
D_KV = H_KV * HEAD_DIM
D_MIX = D_CONV + D_NA + D_SW
N_BRANCH = 3
IN_COLS = 3 * D_CONV + 3 * D_NA + D_SW + 2 * D_KV + N_BRANCH * D_MODEL
N_GROUPS = 4
EXP_PER_GROUP = 8
N_EXPERTS = N_GROUPS * EXP_PER_GROUP
TOP_K = 2
D_EXPERT = 256
MOE_BLK = 256
EPS = 1e-6
NEG_INF = -1e30

kernel_name = "hybrid_conv_natten_swa_hmoe_dit"

def rmsnorm(x, g):
    xf = x.astype(jnp.float32)
    y = xf * lax.rsqrt(jnp.mean(xf * xf, axis=-1, keepdims=True) + EPS)
    return (y * g.astype(jnp.float32)).astype(x.dtype)

def modln(x, g, shift, scale):
    return rmsnorm(x, g) * (1 + scale) + shift

def heads(t, n):
    return t.reshape(t.shape[:-1] + (n, HEAD_DIM))

def split_in(u):
    sizes = (D_CONV, D_CONV, D_CONV, D_NA, D_NA, D_NA, D_SW, D_KV, D_KV, N_BRANCH * D_MODEL)
    idx, acc = [], 0
    for s in sizes[:-1]:
        acc += s
        idx.append(acc)
    return jnp.split(u, idx, axis=-1)

def axial_rope(x, row, col):
    half = HEAD_DIM // 2
    quarter = half // 2
    inv = ROPE_BASE ** (-jnp.arange(quarter, dtype=jnp.float32) / quarter)

    def rot(xa, pos):
        ang = pos[:, None] * inv[None, :]
        cos = jnp.cos(ang)[:, None, :]
        sin = jnp.sin(ang)[:, None, :]
        x1, x2 = jnp.split(xa, 2, axis=-1)
        return jnp.concatenate([x1 * cos - x2 * sin, x1 * sin + x2 * cos], axis=-1)

    xf = x.astype(jnp.float32)
    out = jnp.concatenate([rot(xf[..., :half], row), rot(xf[..., half:], col)], axis=-1)
    return out.astype(x.dtype)

def short_conv(h, b_gate, c_gate, w):
    z = c_gate * h
    pad = CONV_W // 2
    n = z.shape[1]
    zp = jnp.pad(z, ((0, 0), (pad, pad), (0, 0)))
    y = zp[:, 0:n] * w[0]
    for j in range(1, CONV_W):
        y = y + zp[:, j:j + n] * w[j]
    return b_gate * y

def ctx_attn(q, k, v, sink):
    bsz, n, hq, dh = q.shape
    hkv = k.shape[2]
    g = hq // hkv
    qg = q.reshape(bsz, n, hkv, g, dh)
    s = jnp.einsum('bqkgd,bjkd->bkgqj', qg, k).astype(jnp.float32) * (dh ** -0.5)
    if sink is not None:
        sink_col = jnp.broadcast_to(sink.astype(jnp.float32).reshape(1, hkv, g, 1, 1), (bsz, hkv, g, n, 1))
        s = jnp.concatenate([s, sink_col], axis=-1)
    p = jax.nn.softmax(s, axis=-1)[..., :n].astype(v.dtype)
    o = jnp.einsum('bkgqj,bjkd->bqkgd', p, v)
    return o.reshape(bsz, n, hq * dh)

def neighbourhood_attn(q, k, v, kc, vc, rpb):
    bsz, n, h, dh = q.shape
    rows = n // GRID_W
    win_r = min(WIN_R_MAX, rows)
    nw = win_r * WIN_C
    scale = dh ** -0.5
    kg = k.reshape(bsz, rows, GRID_W, h, dh)
    vg = v.reshape(bsz, rows, GRID_W, h, dh)
    qg = q.reshape(bsz, rows, GRID_W, h, dh).transpose(1, 0, 2, 3, 4)
    cols = jnp.arange(GRID_W)
    cstart = jnp.clip(cols - WIN_C // 2, 0, GRID_W - WIN_C)
    col_idx = cstart[:, None] + jnp.arange(WIN_C)[None, :]
    rel_c = col_idx - cols[:, None] + (WIN_C - 1)

    def one_row(args):
        r, q_row = args
        rs = jnp.clip(r - win_r // 2, 0, rows - win_r)
        kb = lax.dynamic_slice_in_dim(kg, rs, win_r, axis=1)
        vb = lax.dynamic_slice_in_dim(vg, rs, win_r, axis=1)
        kw = kb[:, :, col_idx]
        vw = vb[:, :, col_idx]
        rel_r = rs + jnp.arange(win_r) - r + (WIN_R_MAX - 1)
        bias = rpb[:, rel_r[None, :, None], rel_c[:, None, :]]
        s_win = jnp.einsum('bqhd,baqchd->bhqac', q_row, kw).astype(jnp.float32) * scale
        s_win = (s_win + bias.astype(jnp.float32)[None]).reshape(bsz, h, GRID_W, nw)
        s_ctx = jnp.einsum('bqhd,bnhd->bhqn', q_row, kc).astype(jnp.float32) * scale
        p = jax.nn.softmax(jnp.concatenate([s_win, s_ctx], axis=-1), axis=-1).astype(q.dtype)
        p_win = p[..., :nw].reshape(bsz, h, GRID_W, win_r, WIN_C)
        o = jnp.einsum('bhqac,baqchd->bqhd', p_win, vw) + jnp.einsum('bhqn,bnhd->bqhd', p[..., nw:], vc)
        return o

    out = lax.map(one_row, (jnp.arange(rows), qg))
    return out.transpose(1, 0, 2, 3, 4).reshape(bsz, n, h * dh)

def window_attn(q, k, v, kc, vc, sink):
    bsz, n, hq, dh = q.shape
    hkv = k.shape[2]
    g = hq // hkv
    nctx = kc.shape[1]
    nblk = n // BLK_Q
    span = BLK_Q + 2 * WINDOW
    scale = dh ** -0.5
    kp = jnp.pad(k, ((0, 0), (WINDOW, WINDOW), (0, 0), (0, 0)))
    vp = jnp.pad(v, ((0, 0), (WINDOW, WINDOW), (0, 0), (0, 0)))
    qb = q.reshape(bsz, nblk, BLK_Q, hkv, g, dh).transpose(1, 0, 2, 3, 4, 5)
    sink_col = jnp.broadcast_to(sink.astype(jnp.float32).reshape(1, hkv, g, 1, 1), (bsz, hkv, g, BLK_Q, 1))

    def one_block(args):
        b, q_blk = args
        start = b * BLK_Q
        kw = lax.dynamic_slice_in_dim(kp, start, span, axis=1)
        vw = lax.dynamic_slice_in_dim(vp, start, span, axis=1)
        qpos = start + jnp.arange(BLK_Q)
        kpos = start - WINDOW + jnp.arange(span)
        valid = (jnp.abs(qpos[:, None] - kpos[None, :]) <= WINDOW) & (kpos >= 0)[None, :] & (kpos < n)[None, :]
        s_win = jnp.einsum('bqkgd,bjkd->bkgqj', q_blk, kw).astype(jnp.float32) * scale
        s_win = jnp.where(valid, s_win, NEG_INF)
        s_ctx = jnp.einsum('bqkgd,bckd->bkgqc', q_blk, kc).astype(jnp.float32) * scale
        p = jax.nn.softmax(jnp.concatenate([s_win, s_ctx, sink_col], axis=-1), axis=-1).astype(q.dtype)
        o = jnp.einsum('bkgqj,bjkd->bqkgd', p[..., :span], vw) + jnp.einsum('bkgqc,bckd->bqkgd', p[..., span:span + nctx], vc)
        return o.reshape(bsz, BLK_Q, hq * dh)

    out = lax.map(one_block, (jnp.arange(nblk), qb))
    return out.transpose(1, 0, 2, 3).reshape(bsz, n, hq * dh)

def merge_branches(y_a, y_b, y_c, gate_logits, w_branch, w_o):
    g_a, g_b, g_c = jnp.split(jax.nn.sigmoid(gate_logits), N_BRANCH, axis=-1)
    o1 = D_CONV
    o2 = D_CONV + D_NA
    m = g_a * (y_a @ w_branch[:o1]) + g_b * (y_b @ w_branch[o1:o2]) + g_c * (y_c @ w_branch[o2:])
    return m @ w_o

def token_mixers(h, hc, w_in, conv_w, rpb, sink, w_branch, w_o, row, col, need_ctx):
    a_h, a_b, a_c, nq, nk, nv, wq, wk, wv, gates = split_in(h @ w_in)
    ca_h, ca_b, ca_c, cnq, cnk, cnv, cwq, cwk, cwv, cgates = split_in(hc @ w_in)
    cnk, cnv = heads(cnk, H_NA), heads(cnv, H_NA)
    cwk, cwv = heads(cwk, H_KV), heads(cwv, H_KV)
    y_a = short_conv(a_h, a_b, a_c, conv_w)
    y_b = neighbourhood_attn(heads(nq, H_NA), heads(nk, H_NA), heads(nv, H_NA), cnk, cnv, rpb)
    y_c = window_attn(axial_rope(heads(wq, H_Q), row, col), axial_rope(heads(wk, H_KV), row, col),
                      heads(wv, H_KV), cwk, cwv, sink)
    y = merge_branches(y_a, y_b, y_c, gates, w_branch, w_o)
    if not need_ctx:
        return y, None
    yc_a = short_conv(ca_h, ca_b, ca_c, conv_w)
    yc_b = ctx_attn(heads(cnq, H_NA), cnk, cnv, None)
    yc_c = ctx_attn(heads(cwq, H_Q), cwk, cwv, sink)
    yc = merge_branches(yc_a, yc_b, yc_c, cgates, w_branch, w_o)
    return y, yc

def hier_moe(xt, w_rg, b_rg, w_re, b_re, w_g, w_u, w_d):
    n, d = xt.shape
    lg = (xt @ w_rg + b_rg).astype(jnp.float32)
    pg = jax.nn.softmax(lg, axis=-1)
    gi = jnp.argmax(lg, axis=-1)
    pg_top = jnp.take_along_axis(pg, gi[:, None], axis=-1)[:, 0]
    le = (xt @ w_re + b_re).astype(jnp.float32).reshape(n, N_GROUPS, EXP_PER_GROUP)
    le_g = jnp.take_along_axis(le, gi[:, None, None], axis=1)[:, 0]
    top_v, top_i = lax.top_k(le_g, TOP_K)
    wts = (pg_top[:, None] * jax.nn.softmax(top_v, axis=-1)).reshape(-1)
    eid = (gi[:, None] * EXP_PER_GROUP + top_i).reshape(-1).astype(jnp.int32)
    tok = jnp.repeat(jnp.arange(n), TOP_K)
    a = n * TOP_K
    order = jnp.argsort(eid)
    e_s, t_s, w_s = eid[order], tok[order], wts[order]
    counts = jnp.bincount(eid, length=N_EXPERTS)
    padded = ((counts + MOE_BLK - 1) // MOE_BLK) * MOE_BLK
    seg_start = jnp.cumsum(counts) - counts
    pad_end = jnp.cumsum(padded)
    pad_start = pad_end - padded
    dest = pad_start[e_s] + jnp.arange(a) - seg_start[e_s]
    nb = (a + N_EXPERTS * (MOE_BLK - 1) + MOE_BLK - 1) // MOE_BLK
    xd = jnp.zeros((nb * MOE_BLK, d), xt.dtype).at[dest].set(xt[t_s])
    blk_start = jnp.arange(nb) * MOE_BLK
    blk_e = jnp.clip(jnp.sum(pad_end[None, :] <= blk_start[:, None], axis=1), 0, N_EXPERTS - 1)

    def expert_block(args):
        xb, e = args
        hid = jax.nn.silu(xb @ w_g[e]) * (xb @ w_u[e])
        return hid @ w_d[e]

    yd = lax.map(expert_block, (xd.reshape(nb, MOE_BLK, d), blk_e)).reshape(nb * MOE_BLK, d)
    return jnp.zeros((n, d), xt.dtype).at[t_s].add(yd[dest] * w_s[:, None].astype(xt.dtype))

def setup_inputs(seed: int = 0) -> dict:
    key = jax.random.key(seed)
    ks = jax.random.split(key, 26)
    f32 = jnp.float32

    def nrm(k, shape, scale):
        return jax.random.normal(k, shape, f32) * scale

    w_branch = jnp.concatenate([
        nrm(ks[12], (DEPTH, D_CONV, D_MODEL), D_CONV ** -0.5),
        nrm(ks[13], (DEPTH, D_NA, D_MODEL), D_NA ** -0.5),
        nrm(ks[14], (DEPTH, D_SW, D_MODEL), D_SW ** -0.5)], axis=1)
    return {
        "x": nrm(ks[0], (BATCH, SEQ, D_MODEL), 1.0),
        "c": nrm(ks[1], (BATCH, D_MODEL), 1.0),
        "ctx": nrm(ks[2], (BATCH, CTX_LEN, D_MODEL), 1.0),
        "c_ctx": nrm(ks[3], (D_MODEL,), 1.0),
        "w_mod": nrm(ks[4], (DEPTH, D_MODEL, 6 * D_MODEL), 0.5 * D_MODEL ** -0.5),
        "b_mod": nrm(ks[5], (DEPTH, 6 * D_MODEL), 0.02),
        "g_attn": 1.0 + nrm(ks[6], (DEPTH, D_MODEL), 0.05),
        "g_ffn": 1.0 + nrm(ks[7], (DEPTH, D_MODEL), 0.05),
        "w_in": nrm(ks[8], (DEPTH, D_MODEL, IN_COLS), D_MODEL ** -0.5),
        "conv_w": nrm(ks[9], (DEPTH, CONV_W, D_CONV), CONV_W ** -0.5),
        "rpb": nrm(ks[10], (DEPTH, H_NA, 2 * WIN_R_MAX - 1, 2 * WIN_C - 1), 0.1),
        "sinks": nrm(ks[11], (DEPTH, H_Q), 0.5),
        "w_branch": w_branch,
        "w_o": nrm(ks[15], (DEPTH, D_MODEL, D_MODEL), D_MODEL ** -0.5),
        "w_rg": nrm(ks[16], (DEPTH, D_MODEL, N_GROUPS), D_MODEL ** -0.5),
        "b_rg": nrm(ks[17], (DEPTH, N_GROUPS), 0.01),
        "w_re": nrm(ks[18], (DEPTH, D_MODEL, N_EXPERTS), D_MODEL ** -0.5),
        "b_re": nrm(ks[19], (DEPTH, N_EXPERTS), 0.01),
        "w_e_gate": nrm(ks[20], (DEPTH, N_EXPERTS, D_MODEL, D_EXPERT), D_MODEL ** -0.5),
        "w_e_up": nrm(ks[21], (DEPTH, N_EXPERTS, D_MODEL, D_EXPERT), D_MODEL ** -0.5),
        "w_e_down": nrm(ks[22], (DEPTH, N_EXPERTS, D_EXPERT, D_MODEL), D_EXPERT ** -0.5),
        "g_final": 1.0 + nrm(ks[23], (D_MODEL,), 0.05),
    }

def reference(x, c, ctx, c_ctx, w_mod, b_mod, g_attn, g_ffn, w_in, conv_w, rpb, sinks,
              w_branch, w_o, w_rg, b_rg, w_re, b_re, w_e_gate, w_e_up, w_e_down, g_final):
    bsz, n, d = x.shape
    t = jnp.arange(n)
    row = (t // GRID_W).astype(jnp.float32)
    col = (t % GRID_W).astype(jnp.float32)
    silu_c = jax.nn.silu(c)
    silu_cc = jax.nn.silu(c_ctx)
    xc = ctx
    for l in range(DEPTH):
        need_ctx = l < DEPTH - 1
        mod = (silu_c @ w_mod[l] + b_mod[l])[:, None, :]
        modc = silu_cc @ w_mod[l] + b_mod[l]
        sh_a, sc_a, gt_a, sh_f, sc_f, gt_f = jnp.split(mod, 6, axis=-1)
        csh_a, csc_a, cgt_a, csh_f, csc_f, cgt_f = jnp.split(modc, 6, axis=-1)
        h = modln(x, g_attn[l], sh_a, sc_a)
        hc = modln(xc, g_attn[l], csh_a, csc_a)
        y, yc = token_mixers(h, hc, w_in[l], conv_w[l], rpb[l], sinks[l], w_branch[l], w_o[l], row, col, need_ctx)
        x = x + gt_a * y
        h2 = modln(x, g_ffn[l], sh_f, sc_f)
        if need_ctx:
            xc = xc + cgt_a * yc
            h2c = modln(xc, g_ffn[l], csh_f, csc_f)
            toks = jnp.concatenate([h2.reshape(-1, d), h2c.reshape(-1, d)], axis=0)
            yt = hier_moe(toks, w_rg[l], b_rg[l], w_re[l], b_re[l], w_e_gate[l], w_e_up[l], w_e_down[l])
            nl = bsz * n
            x = x + gt_f * yt[:nl].reshape(x.shape)
            xc = xc + cgt_f * yt[nl:].reshape(xc.shape)
        else:
            yt = hier_moe(h2.reshape(-1, d), w_rg[l], b_rg[l], w_re[l], b_re[l], w_e_gate[l], w_e_up[l], w_e_down[l])
            x = x + gt_f * yt.reshape(x.shape)
    return rmsnorm(x, g_final)


_drawn_inputs = setup_inputs


def setup_inputs(seed=0):
    import zlib

    import numpy as np

    out = dict(_drawn_inputs(seed))
    spreads = {}
    factors = {'rpb': 23.741, 'sinks': 40.637, 'b_rg': 28.707, 'b_re': 7.946}
    for name, (base, spread) in spreads.items():
        noise = np.random.default_rng([zlib.crc32(name.encode()), seed]).standard_normal(out[name].shape)
        drawn = base * np.exp(spread * noise) if base else spread * noise
        out[name] = __import__('jax').numpy.asarray(drawn.astype(out[name].dtype))
    for name, factor in factors.items():
        out[name] = (out[name] * factor).astype(out[name].dtype)
    return out
```

```python
from contextlib import ExitStack

import numpy as np
import concourse.bass as bass
from concourse import mybir

P = 128
D = 1024
KD = D // P
SEQ, CTX, DEPTH = 256, 256, 2
NTOK = SEQ + CTX
GRID_W, HD, D_CONV, CONV_W = 64, 64, 256, 3
H_NA, WIN_R_MAX, WIN_C = 6, 8, 16
H_Q, H_KV, WINDOW = 6, 2, 128
D_NA, D_SW, D_KV = H_NA * HD, H_Q * HD, H_KV * HD
COL_NQ = 3 * D_CONV
COL_NV = COL_NQ + 2 * D_NA
COL_WQ = COL_NV + D_NA
COL_WK = COL_WQ + D_SW
COL_WV = COL_WK + D_KV
COL_G = COL_WV + D_KV
NG, EPG = 4, 8
NE = NG * EPG
NR = NG + NE
DE = 256
EPS = 1e-6
NEG = -1e30
ROPE_BASE = 10000.0
RPB_R, RPB_C = 2 * WIN_R_MAX - 1, 2 * WIN_C - 1
ROWS = SEQ // GRID_W
SCALE = HD ** -0.5

CW = 256
SLOTS = 9
UNROLL = 3
CAP = 64
MAIN = NE * CAP
SPILL = [2 * NTOK // CAP, 2 * SEQ // CAP]
ROWS_D = MAIN + SPILL[0] * CAP
NBK = NTOK // CAP

F32 = mybir.dt.float32
I32 = mybir.dt.int32
U32 = mybir.dt.uint32
ALU = mybir.AluOpType
ACT = mybir.ActivationFunctionType
AX = mybir.AxisListType

CONST_COLS = dict(ident=P, upper=P, ones=P, rot=P, flip=P, cos=SEQ, sin=SEQ, mask_na=GRID_W,
                  mask_win=2 * SEQ, iota=NE, slot0=NE, thr=NBK - 1)


def constants():
    p = np.arange(P)
    c = {"ident": np.eye(P), "ones": np.ones((P, P)),
         "upper": (p[:, None] < p[None, :]).astype(np.float32)}
    rot = np.zeros((P, P))
    for m in range(P):
        if m % 32 < 16:
            rot[m + 16, m] = -1.0
        else:
            rot[m - 16, m] = 1.0
    c["rot"] = rot
    flip = np.zeros((P, P))
    flip[(p // 64) * 64 + 63 - p % 64, p] = 1.0
    c["flip"] = flip
    t = np.arange(SEQ)
    quarter = HD // 4
    inv = np.float32(ROPE_BASE) ** (-np.arange(quarter, dtype=np.float32) / np.float32(quarter))
    pos = np.where((p % HD < HD // 2)[:, None], (t // GRID_W)[None], (t % GRID_W)[None])
    ang = pos.astype(np.float32) * inv[p % quarter][:, None].astype(np.float32)
    c["cos"], c["sin"] = np.cos(ang), np.sin(ang)
    col = p % GRID_W
    start = np.clip(col - WIN_C // 2, 0, GRID_W - WIN_C)
    kc = np.arange(GRID_W)[None]
    c["mask_na"] = np.where((kc >= start[:, None]) & (kc < start[:, None] + WIN_C), 0.0, NEG)
    k = np.arange(SEQ)[None]
    c["mask_win"] = np.concatenate(
        [np.where(np.abs(k - (b * P + p)[:, None]) <= WINDOW, 0.0, NEG) for b in range(2)], 1)
    c["iota"] = np.tile(np.arange(NE), (P, 1))
    c["slot0"] = np.tile(np.arange(NE) * CAP, (P, 1))
    c["thr"] = np.tile(np.arange(1, NBK) * CAP, (P, 1))
    return np.concatenate([c[n].astype(np.float32) for n in CONST_COLS], axis=1)


def weight_stream():
    out = []
    for l in range(DEPTH):
        if l == 0:
            out += [("mod", 0, c) for c in range(12)]
        out += [("in", l, c) for c in range(10)]
        for n in range(4):
            out += [("gate", l, 3 * n + b) for b in range(3)] + [("branch", l, n)]
        out += [("wo", l, c) for c in range(4)]
        out += [("mod", l, c) for c in range(12, 24)]
        if l == 0:
            out += [("mod", 1, c) for c in range(12)]
        out += [("eg", l, 0), ("eu", l, 0)]
        for e in range(NE):
            if e + 1 < NE:
                out += [("eg", l, e + 1), ("eu", l, e + 1)]
            out += [("ed", l, e)]
    return out


PIECES = {("in", 7): 2, ("in", 8): 4, ("in", 9): 3}


def pieces(kind, index):
    if kind == "branch":
        return 3
    return PIECES.get((kind, index), 1)


STREAM = weight_stream()
AT = {key: j for j, key in enumerate(STREAM)}
LOADED = []
for _j, (_k, _l, _i) in enumerate(STREAM):
    LOADED.append((LOADED[_j - SLOTS] if _j >= SLOTS else 0) + 16 * pieces(_k, _i))


T_AH, T_AB, T_AC, T_NQ, T_WQ, T_NK, T_WK = 0, 2, 4, 6, 9, 12, 15
IN_TILES = {0: (0, 1), 1: (2, 3), 2: (4, 5), 3: (6, 7), 4: (8, 12), 5: (13, 14), 8: (9, 10), 9: (11, 15)}


def proj_outputs(l):
    out = [("bias", h, None) for h in range(H_NA)]
    for c in range(10):
        if c in IN_TILES:
            out += [("chan", c, t) for t in enumerate(IN_TILES[c])]
        else:
            out += [("val", c, tt) for tt in range(4)]
    return out


OUTS = [proj_outputs(l) for l in range(DEPTH)]
N_OUT = len(OUTS[0])


def by_act(o):
    return OUTS[0][o][0] != "bias" and o % 2 == 0


N_ACT_OUT = sum(by_act(o) for o in range(N_OUT))
N_DVE_OUT = N_OUT - N_ACT_OUT


def out_count(l, o):
    mine = by_act(o)
    n = sum(by_act(q) == mine for q in range(o + 1))
    return mine, n + l * (N_ACT_OUT if mine else N_DVE_OUT)


def last_out(l, c):
    return l * N_OUT + 1 + max(o for o, x in enumerate(OUTS[l]) if x[0] != "bias" and x[1] == c)


def steps(l):
    out = [("na", h, False) for h in range(H_NA)] + [("win", h, False) for h in range(H_Q)]
    if l < DEPTH - 1:
        out += [("na", h, True) for h in range(H_NA)] + [("win", h, True) for h in range(H_Q)]
    return out


STEPS = [steps(l) for l in range(DEPTH)]
STEP0 = [0, len(STEPS[0])]
QT = [4, 2]
QN = [q * P for q in QT]
QT0 = [0, 4]


def lat_steps(l, s):
    return sum(not x[2] for k in range(l) for x in STEPS[k]) + sum(not x[2] for x in STEPS[l][:s + 1])


def width(l, s):
    family, _, on_ctx = STEPS[l][s]
    return (CTX if on_ctx else NTOK) + (family == "win")


SMALL = 16 * 6


def lin(i, first, per):
    return first if i is None else i * per + first


def program(nc, t, out):
    ctx = ExitStack()
    with ctx:
        def sb(name, shape, dt=F32):
            return ctx.enter_context(nc.sbuf_tensor(name, shape, dt))

        def sem(name):
            return ctx.enter_context(nc.semaphore(name))

        xd = nc.dram_tensor("dispatched", (ROWS_D, D), F32, kind="Internal").ap()
        yd = nc.dram_tensor("expert_rows", (ROWS_D, D), F32, kind="Internal").ap()

        consts = sb("consts", [P, sum(CONST_COLS.values())])
        at, C = 0, {}
        for name, n in CONST_COLS.items():
            C[name] = consts[:, at:at + n]
            at += n
        ident = C["ident"]
        ring = sb("ring", [P, SLOTS, KD * CW])
        X = sb("X", [P, 4, D])
        hT = sb("hT", [P, KD, NTOK])
        arena = sb("arena", [P, 20, 512])
        modc = sb("modc", [P, 3, D])
        strip = sb("strip", [P, H_NA, 6 * GRID_W])
        att = sb("att", [P, 3 * 2 * 516 + 1024])
        cond = sb("cond", [P, 2, KD])
        cond_s = sb("cond_s", [P, 2, KD])
        cond_bc = sb("cond_bc", [P, KD, P])
        w_router = sb("w_router", [P, KD, NR])
        b_router = sb("b_router", [P, NR])
        sinks_bc = sb("sinks_bc", [P, H_Q])
        convw = sb("convw", [P, 2, CONV_W])
        stat = sb("stat", [P, 24])
        negmax = sb("negmax", [P, 3, 2])
        esum = sb("esum", [P, 3, 2])
        rsum = sb("rsum", [P, 3, 2])
        top_g = sb("top_g", [P, 4, 8])
        idx_g = sb("idx_g", [P, 4, 8], U32)
        top_e = sb("top_e", [P, 4, 8])
        idx_e = sb("idx_e", [P, 4, 8], U32)
        rt = sb("rt", [P, 64])
        slots_f = sb("slots_f", [P, 2, 4])
        slots_u = sb("slots_u", [P, 2, 4], U32)
        wts = sb("wts", [P, 2, 4])
        meta = sb("meta", [1, 1 + SPILL[0]], I32)

        def tile(n, k=1):
            return arena[:, n:n + k, :].rearrange("p a b -> p (a b)")

        vals = arena[:, 16:20, :]
        htok = arena[:, 12:20, :].rearrange("p (t a) b -> p t (a b)", a=2)
        mT = arena[:, 12:20, :]
        mod_scale = [tile(0, 2), tile(4, 2)]
        mod_shift = [tile(2, 2), tile(6, 2)]
        gate_bc = [tile(0, 2), tile(2, 2)]
        gate_f = [tile(4, 2), tile(6, 2)]
        g_bc = strip[:, :, :].rearrange("p a b -> p (a b)")[:, 0:D]
        xe = [arena[0:CAP, 8 + 2 * b:10 + 2 * b, :].rearrange("p a b -> p (a b)") for b in range(2)]
        xe.append(arena[0:CAP, 14:16, :].rearrange("p a b -> p (a b)"))
        xeT = [arena[:, b, :].rearrange("p (k s) -> p k s", k=KD) for b in range(3)]
        act_g = arena[0:CAP, 3, 0:DE]
        hid = arena[0:CAP, 3, DE:2 * DE]
        y_sb = arena[0:CAP, 12:14, :].rearrange("p a b -> p (a b)")
        hidT = sb("hidT", [P, 2, CAP])
        spill_gu = [hT[:, 4 * b:4 * b + 4, :].rearrange("p a b -> p (a b)") for b in range(2)]
        spill_d = arena[:, 16:20, :].rearrange("p a b -> p (a b)")
        S = [att[:, 1032 * b:1032 * b + 1032].rearrange("p (t c) -> p t c", t=2) for b in range(3)]
        PT = att[:, 3096:4120].rearrange("p (k q) -> p k q", k=4)
        rev = att[:, 0:H_NA * 6 * GRID_W]
        sig = [att[:, 512 * b:512 * b + 512] for b in range(6)]
        got = [[att[:, 2048 * b + 1024 * j:2048 * b + 1024 * j + 1024] for j in range(2)] for b in range(2)]
        pick = att[:, 0:256].rearrange("p (c t e) -> p c t e", c=2, t=4)
        prod = att[:, 256:512].rearrange("p (c t e) -> p c t e", c=2, t=4)
        both = att[:, 512:640].rearrange("p (t e) -> p t e", t=4)
        rank = att[:, 640:768].rearrange("p (t e) -> p t e", t=4)
        lem = att[:, 768:896].rearrange("p (t e) -> p t e", t=4)
        cnt = att[:, 896:1024]
        lg = att[:, 1024:1024 + 4 * NR].rearrange("p (t e) -> p t e", t=4)
        g8 = att[:, 1280:1312].rearrange("p (t e) -> p t e", t=4)
        rope_t = att[:, 2304:2304 + 4 * SEQ].rearrange("p (a b) -> p a b", a=4)
        upd = [att[:, 3072:3328], att[:, 3328:3584], att[:, 3584:3840], att[:, 3840:4096]]

        banks = ctx.enter_context(nc.psum_tensor("banks", [P, 8, 512], F32))

        consts_in = sem("consts_in")
        cond_in = sem("cond_in")
        x_in = sem("x_in")
        small_in = [sem(f"small_in{l}") for l in range(DEPTH)]
        bias_in = [sem(f"bias_in{s}") for s in range(3)]
        g_in = sem("g_in")
        rev_in = sem("rev_in")
        loaded = [sem(f"loaded{s}") for s in range(SLOTS)]
        cond_act = sem("cond_act")
        cond_ready = sem("cond_ready")
        mod_done = sem("mod_done")
        mod_out = sem("mod_out")
        scale_ready = sem("scale_ready")
        shift_ready = sem("shift_ready")
        rstd_ready = sem("rstd_ready")
        sq_done = sem("sq_done")
        ms_ready = sem("ms_ready")
        std_ready = sem("std_ready")
        h_scaled = sem("h_scaled")
        h_ready = sem("h_ready")
        h_turned = sem("h_turned")
        hT_act = sem("hT_act")
        hT_dve = sem("hT_dve")
        proj_done = sem("proj_done")
        out_act = sem("out_act")
        out_dve = sem("out_dve")
        rope_mm = sem("rope_mm")
        rope_done = sem("rope_done")
        z_ready = sem("z_ready")
        conv_done = sem("conv_done")
        y_a_ready = sem("y_a_ready")
        sc_done = sem("sc_done")
        s_dve = sem("s_dve")
        s_act = sem("s_act")
        max_ready = sem("max_ready")
        exp_done = sem("exp_done")
        p_ready = sem("p_ready")
        p_turned = sem("p_turned")
        pt_dve = sem("pt_dve")
        pt_act = sem("pt_act")
        pv_done = sem("pv_done")
        o_ready = sem("o_ready")
        gate_done = sem("gate_done")
        branch_done = sem("branch_done")
        sig_ready = sem("sig_ready")
        gated = sem("gated")
        m_ready = sem("m_ready")
        wo_done = sem("wo_done")
        gate_ready = sem("gate_ready")
        upd_ready = sem("upd_ready")
        x_attn = sem("x_attn")
        x_moe = sem("x_moe")
        lg_done = sem("lg_done")
        router_exp_in = sem("router_exp_in")
        router_exp = sem("router_exp")
        pick_ready = sem("pick_ready")
        rank_done = sem("rank_done")
        slots_ready = sem("slots_ready")
        wts_ready = sem("wts_ready")
        zero_ready = sem("zero_ready")
        xd_zero = sem("xd_zero")
        scattered = sem("scattered")
        xe_in = [sem(f"xe_in{b}") for b in range(3)]
        xe_turned = sem("xe_turned")
        xeT_ready = sem("xeT_ready")
        e_gate_done = sem("e_gate_done")
        e_up_done = sem("e_up_done")
        silu_ready = sem("silu_ready")
        hid_ready = sem("hid_ready")
        hid_turned = sem("hid_turned")
        hidT_ready = sem("hidT_ready")
        down_done = sem("down_done")
        y_out = sem("y_out")
        y_stored = sem("y_stored")
        spill_dma = [sem(f"spill_dma{l}") for l in range(DEPTH)]
        spill_out = [sem(f"spill_out{l}") for l in range(DEPTH)]
        spill_step = [sem(f"spill_step{l}") for l in range(DEPTH)]
        rows_done = sem("rows_done")
        got_in = [sem("got_in0"), sem("got_in1")]
        gate_f_ready = sem("gate_f_ready")
        y_gated = sem("y_gated")
        fin_ready = sem("fin_ready")
        stored = sem("stored")
        dve_seq = sem("dve_seq")
        pe_held = sem("pe_held")
        act_seq = sem("act_seq")
        pool_seq = sem("pool_seq")

        def chunk(key):
            return ring[:, AT[key] % SLOTS, :].rearrange("p (k n) -> p k n", n=CW)

        def landed(eng, key, i=None):
            j = AT[key]
            eng.wait_ge(loaded[j % SLOTS], lin(i, LOADED[j], 16))

        NORM_TILES = [[0, 1, 2, 3], [0, 1, 2, 3], [0, 1, 2, 3], [0, 1]]
        N0 = [0, 4, 8, 12, 14]

        E0 = [0, NE]
        ZEROED = 16 * (ROWS_D // P + (ROWS_D - MAIN) // P)

        def out_place(l, what, c, arg):
            if what == "val":
                return vals[:, arg, (c - 6) * CW:(c - 5) * CW], CW
            n = NTOK if arg[1] >= T_NK else QN[l]
            return arena[:, arg[1], 0:n], n

        block = ctx.enter_context(nc.Block())

        @block.sync
        def _(sp):
            def released(key, i=None):
                kind, l, c = key
                if kind == "mod":
                    return mod_done, 24 * l + c + 1
                if kind == "in":
                    return proj_done, last_out(l, c)
                if kind == "gate":
                    n, b = divmod(c, 3)
                    return gate_done, 24 * l + 6 * n + 2 * b + 2
                if kind == "branch":
                    return branch_done, 24 * l + 6 * c + 6
                if kind == "wo":
                    return wo_done, 4 * QT0[l] + QT[l] * (c + 1)
                if kind == "eg":
                    return e_gate_done, lin(i, E0[l] + c + 1, UNROLL)
                if kind == "eu":
                    return e_up_done, lin(i, E0[l] + c + 1, UNROLL)
                return down_done, lin(i, E0[l] + c + 1, UNROLL)

            def load(j, i=None, e=None):
                kind, l, c = STREAM[j]
                dst = chunk(STREAM[j])
                if j >= SLOTS:
                    sp.wait_ge(*released(STREAM[j - SLOTS], i))
                done = loaded[j % SLOTS]
                if kind == "mod":
                    src = t["w_mod"][l].rearrange("(p k) n -> p k n", k=KD)[:, :, c * CW:(c + 1) * CW]
                    sp.dma_start(dst, src).then_inc(done, 16)
                elif kind in ("in", "gate"):
                    src = t["w_in"][l].rearrange("(p k) n -> p k n", k=KD)
                    if kind == "gate":
                        n, b = divmod(c, 3)
                        a = COL_G + b * D + n * CW
                        parts = [(0, a, CW)]
                    elif c <= 5:
                        parts = [(0, c * CW, CW)]
                    elif c == 6:
                        parts = [(0, COL_NV, CW)]
                    elif c == 7:
                        parts = [(0, COL_NV + CW, P), (P, COL_WV, P)]
                    else:
                        heads = [(0, 0), (0, 1), (1, 0), (1, 1)] if c == 8 else [(2, 0), (2, 1)]
                        parts = [(n * HD, COL_WQ + (g * 3 + tt) * HD, HD) for n, (tt, g) in enumerate(heads)]
                        if c == 9:
                            parts.append((P, COL_WK, P))
                    assert len(parts) == pieces(kind, c)
                    for to, fr, n in parts:
                        sp.dma_start(dst[:, :, to:to + n], src[:, :, fr:fr + n]).then_inc(done, 16)
                elif kind == "branch":
                    w = t["w_branch"][l][:, c * CW:(c + 1) * CW]
                    o2 = D_CONV + D_NA
                    sp.dma_start(dst[:, 0:5, :], w[0:o2].rearrange("(k p) n -> p k n", p=P)).then_inc(done, 16)
                    for g in range(2):
                        rows = w[o2 + g * 3 * HD:o2 + (g + 1) * 3 * HD]
                        sp.dma_start(dst[g * HD:(g + 1) * HD, 5:8, :],
                                     rows.rearrange("(t r) n -> r t n", r=HD)).then_inc(done, 16)
                elif kind == "wo":
                    src = t["w_o"][l].rearrange("(k p) n -> p k n", p=P)[:, :, c * CW:(c + 1) * CW]
                    sp.dma_start(dst, src).then_inc(done, 16)
                else:
                    name = {"eg": "w_e_gate", "eu": "w_e_up", "ed": "w_e_down"}[kind]
                    w = t[name][l, c] if e is None else t[name][l][bass.ds(e, 1)].rearrange("a r n -> (a r) n")
                    sp.dma_start(ring[:, j % SLOTS, :], w.rearrange("(p k) n -> p (k n)", p=P)).then_inc(done, 16)

            j = 0
            for l in range(DEPTH):
                first = AT[("eg", l, 4)]
                while j < first:
                    load(j)
                    j += 1
                with sp.Fori(0, 9) as i:
                    for u in range(UNROLL):
                        e1, e0 = sp.snap(i * UNROLL + (4 + u)), sp.snap(i * UNROLL + (3 + u))
                        load(j, i, e1)
                        load(j + 1, i, e1)
                        load(j + 2, i, e0)
                        j += 3
                j = AT[("eg", l, 31)]
                last = AT[("ed", l, NE - 1)]
                while j <= last:
                    load(j)
                    j += 1
                sp.wait_ge(slots_ready, l + 1)
                n_spill = sp.value_load(meta[0:1, 0:1], min_val=0, max_val=SPILL[l])
                with sp.If(n_spill > 0):
                    with sp.Fori(0, SPILL[l]) as b:
                        with sp.If(b < n_spill):
                            e = sp.value_load(meta[0:1, bass.ds(b + 1, 1)], min_val=0, max_val=NE - 1)
                            sp.wait_ge(spill_step[l], b * 9 + 1)
                            for dst, name in ((spill_gu[0], "w_e_gate"), (spill_gu[1], "w_e_up"),
                                              (spill_d, "w_e_down")):
                                w = t[name][l][bass.ds(e, 1)].rearrange("a r n -> (a r) n")
                                sp.dma_start(dst, w.rearrange("(p k) n -> p (k n)", p=P)).then_inc(spill_dma[l], 16)
            while j < len(STREAM):
                load(j)
                j += 1

        @block.gpsimd
        def _(pool):
            seq = [0]

            def link(ins):
                seq[0] += 1
                ins.then_inc(pool_seq, 1)
                pool.wait_ge(pool_seq, seq[0])

            def norm_tail(m):
                pool.wait_ge(shift_ready, m + 1)
                for n, tt in enumerate(NORM_TILES[m]):
                    pool.wait_ge(h_scaled, N0[m] + n + 1)
                    pool.tensor_tensor(htok[:, tt, :], htok[:, tt, :], mod_shift[tt // 2], ALU.add)\
                        .then_inc(h_ready, 1)

            def zero_rows():
                zero = tile(T_AC, 2)
                pool.wait_ge(y_a_ready, 2)
                pool.memset(zero, 0.0).then_inc(zero_ready, 1)
                pool.wait_ge(zero_ready, 1)
                for dst, first in ((xd, 0), (yd, MAIN)):
                    for r in range(first // P, ROWS_D // P):
                        pool.dma_start(dst[r * P:(r + 1) * P, :], zero).then_inc(xd_zero, 16)

            def conv(l):
                n = QN[l]
                for o in (10, 11):
                    mine, count = out_count(l, o)
                    pool.wait_ge(out_act if mine else out_dve, count)
                pool.wait_ge(small_in[l], SMALL)
                for c in range(2):
                    a, g = (arena[:, q + c, 0:n] for q in (T_AH, T_AC))
                    link(pool.tensor_tensor(a, a, g, ALU.mult))
                    pool.tensor_scalar(g, a, convw[:, c, 1:2], None, ALU.mult).then_inc(z_ready, 1)
                for c in range(2):
                    pool.wait_ge(conv_done, 2 * l + c + 1)
                    a, b, g = (arena[:, q + c, 0:n] for q in (T_AH, T_AB, T_AC))
                    pool.tensor_tensor(a, g, b, ALU.mult).then_inc(y_a_ready, 1)

            def merge(l):
                n = QN[l]
                pool.wait_ge(pv_done, STEP0[l] + len(STEPS[l]))
                for q in range(8):
                    pair, half = divmod(q, 2)
                    pool.wait_ge(gated, 24 * l + 6 * pair + 3 * half + 3)
                    s = [sig[2 * b + half][:, 0:n] for b in range(3)]
                    link(pool.tensor_tensor(mT[:, q, 0:n], s[0], s[1], ALU.add))
                    pool.tensor_tensor(mT[:, q, 0:n], mT[:, q, 0:n], s[2], ALU.add).then_inc(m_ready, 1)

            def residual(l):
                for c in range(4):
                    for tt in range(QT[l]):
                        r = c * QT[l] + tt
                        pool.wait_ge(upd_ready, 4 * QT0[l] + r + 1)
                        x = X[:, tt, c * CW:(c + 1) * CW]
                        pool.tensor_tensor(x, x, upd[r % 4], ALU.add).then_inc(x_attn, 1)

            def scatter(l):
                pool.wait_ge(slots_ready, l + 1)
                if l == 0:
                    pool.wait_ge(xd_zero, ZEROED)
                for tt in range(QT[l]):
                    for c in range(2):
                        pool.indirect_dma_start(
                            out=xd, out_offset=bass.IndirectOffsetOnAxis(ap=slots_u[:, c, tt:tt + 1], axis=0),
                            in_=htok[:, tt, :], in_offset=None).then_inc(scattered, 16)

            def combine(l):
                pool.wait_ge(y_stored, 16 * (E0[l] + NE))
                pool.wait_ge(rows_done, l + 1)

                def gather(tt):
                    if tt >= 2:
                        pool.wait_ge(x_moe, QT0[l] + tt - 1)
                    for c in range(2):
                        pool.indirect_dma_start(
                            out=got[tt % 2][c], out_offset=None, in_=yd,
                            in_offset=bass.IndirectOffsetOnAxis(ap=slots_u[:, c, tt:tt + 1], axis=0))\
                            .then_inc(got_in[tt % 2], 16)

                gather(0)
                gather(1)
                for tt in range(QT[l]):
                    pool.wait_ge(y_gated, QT0[l] + tt + 1)
                    link(pool.tensor_tensor(X[:, tt, :], X[:, tt, :], got[tt % 2][0], ALU.add))
                    pool.tensor_tensor(X[:, tt, :], X[:, tt, :], got[tt % 2][1], ALU.add).then_inc(x_moe, 1)
                    if tt + 2 < QT[l]:
                        gather(tt + 2)

            for l in range(DEPTH):
                norm_tail(2 * l)
                conv(l)
                if l == 0:
                    zero_rows()
                merge(l)
                residual(l)
                norm_tail(2 * l + 1)
                scatter(l)
                combine(l)

        @block.tensor
        def _(pe):
            mm, turn = nc.tensor.matmul, nc.tensor.transpose

            def mod(l, c):
                if l == 0 and c == 0:
                    pe.wait_ge(cond_ready, 2)
                landed(pe, ("mod", l, c))
                m = 24 * l + c
                if m >= 4:
                    pe.wait_ge(mod_out, m - 3)
                w = chunk(("mod", l, c))
                for k in range(KD):
                    ins = mm(banks[:, 4 + c % 4, 0:CW], cond_bc[:, k, :], w[:, k, :], start=k == 0, stop=k == KD - 1)
                ins.then_inc(mod_done, 1)

            def norm_turn(m):
                if m == 0:
                    pe.wait_ge(consts_in, 16)
                pe.wait_ge(mod_out, 12 * (m + 1))
                for n, tt in enumerate(NORM_TILES[m]):
                    pe.wait_ge(h_ready, N0[m] + n + 1)
                    for half in range(2):
                        for q in range(4):
                            ins = turn(banks[:, 2 * n + half, q * P:(q + 1) * P], htok[:, tt, 4 * half + q::KD], ident)
                        ins.then_inc(h_turned, 1)
                pe.wait_ge(hT_act, N0[m + 1])
                pe.wait_ge(hT_dve, N0[m + 1])

            def project(l):
                for o, (what, c, arg) in enumerate(OUTS[l]):
                    if o >= 8:
                        mine, count = out_count(l, o - 8)
                        pe.wait_ge(out_act if mine else out_dve, count)
                    bank = banks[:, o % 8, :]
                    if what == "bias":
                        if o == 0:
                            pe.wait_ge(rev_in, 16 * 2 * H_NA * (l + 1))
                        ins = mm(bank[:, 0:6 * GRID_W], C["flip"], rev[:, c * 384:(c + 1) * 384], start=True, stop=True)
                    elif what == "chan":
                        half, tn = arg
                        landed(pe, ("in", l, c))
                        w = chunk(("in", l, c))
                        n = NTOK if tn >= T_NK else QN[l]
                        for k in range(KD):
                            ins = mm(bank[:, 0:n], w[:, k, half * P:(half + 1) * P], hT[:, k, 0:n],
                                     start=k == 0, stop=k == KD - 1)
                    else:
                        landed(pe, ("in", l, c))
                        w = chunk(("in", l, c))
                        for k in range(KD):
                            ins = mm(bank[:, 0:CW], hT[:, k, arg * P:(arg + 1) * P], w[:, k, :],
                                     start=k == 0, stop=k == KD - 1)
                    ins.then_inc(proj_done, 1)
                pe.wait_ge(out_act, (l + 1) * N_ACT_OUT)
                pe.wait_ge(out_dve, (l + 1) * N_DVE_OUT)
                for r, tn in enumerate((T_WQ, T_WQ + 1, T_WQ + 2, T_WK)):
                    mm(banks[:, 4 + r, 0:SEQ], C["rot"], arena[:, tn, 0:SEQ], start=True, stop=True).then_inc(rope_mm, 1)

            def q_place(family, h):
                if family == "na":
                    return T_NQ + h // 2, HD * (h % 2)
                return T_WQ + h % 3, HD * (h // 3)

            def scores(l, s):
                family, h, on_ctx = STEPS[l][s]
                g = STEP0[l] + s
                if s >= 2:
                    pe.wait_ge(s_act, g - 1)
                    pe.wait_ge(s_dve, lat_steps(l, s - 2))
                tn, p0 = q_place(family, h)
                kt = T_NK + h // 2 if family == "na" else T_WK
                q0 = SEQ if on_ctx else 0
                for part in ((1,) if on_ctx else (0, 1)):
                    for b in range(2):
                        ins = mm(banks[:, 2 * (s % 2) + part, b * SEQ:(b + 1) * SEQ],
                                 arena[p0:p0 + HD, tn, q0 + b * P:q0 + (b + 1) * P],
                                 arena[p0:p0 + HD, kt, part * SEQ:(part + 1) * SEQ], start=True, stop=True)
                ins.then_inc(sc_done, 1)

            def turn_p(l, s):
                on_ctx = STEPS[l][s][2]
                g = STEP0[l] + s
                pe.wait_ge(p_ready, g + 1)
                if g:
                    pe.wait_ge(pt_dve, g)
                    pe.wait_ge(pt_act, g)
                for b in range(2):
                    for q in range(2 if on_ctx else 4):
                        ins = turn(banks[:, 4 + b, q * P:(q + 1) * P], S[s % 3][:, b, q * P:(q + 1) * P], ident)
                ins.then_inc(p_turned, 1)

            def attend(l, s):
                family, h, on_ctx = STEPS[l][s]
                g = STEP0[l] + s
                pe.wait_ge(pt_dve, g + 1)
                pe.wait_ge(pt_act, g + 1)
                if g >= 2:
                    pe.wait_ge(o_ready, g - 1)
                v0 = h * HD if family == "na" else D_NA + (h // 3) * HD
                t0, n = (2, 2) if on_ctx else (0, 4)
                for q in range(n):
                    ins = mm(banks[0:HD, 6 + s % 2, 0:2 * P], vals[:, t0 + q, v0:v0 + HD], PT[:, q, :],
                             start=q == 0, stop=q == n - 1)
                ins.then_inc(pv_done, 1)

            def attention(l):
                n = len(STEPS[l])
                for s in range(-1, n + 2):
                    if s == 1:
                        pe.wait_ge(rope_done, 4 * (l + 1))
                    if s + 1 < n:
                        scores(l, s + 1)
                    if 0 <= s - 2 < n:
                        attend(l, s - 2)
                    if 0 <= s - 1 < n:
                        turn_p(l, s - 1)

            BRANCH = [(0, 1), (2, 3, 4), (5, 6, 7)]
            Y_TILE = [T_AH, T_AH + 1, T_NQ, T_NQ + 1, T_NQ + 2, T_WQ, T_WQ + 1, T_WQ + 2]

            def merge(l):
                n = QN[l]
                pe.wait_ge(o_ready, STEP0[l] + len(STEPS[l]))
                pe.wait_ge(y_a_ready, 2 * (l + 1))

                def bank(pair, r):
                    q = 12 * pair + r
                    if q >= 8:
                        pr, rr = divmod(q - 8, 12)
                        if rr < 6:
                            pe.wait_ge(sig_ready, 24 * l + 6 * pr + rr + 1)
                        else:
                            pe.wait_ge(gated, 24 * l + 6 * pr + rr - 6 + 1)
                    return banks[:, q % 8, 0:n]

                for pair in range(4):
                    for b in range(3):
                        key = ("gate", l, 3 * pair + b)
                        landed(pe, key)
                        w = chunk(key)
                        for half in range(2):
                            o = bank(pair, 2 * b + half)
                            for k in range(KD):
                                ins = mm(o, w[:, k, half * P:(half + 1) * P], hT[:, k, 0:n],
                                         start=k == 0, stop=k == KD - 1)
                            ins.then_inc(gate_done, 1)
                    landed(pe, ("branch", l, pair))
                    w = chunk(("branch", l, pair))
                    for half in range(2):
                        for b in range(3):
                            o = bank(pair, 6 + 3 * half + b)
                            for k in BRANCH[b]:
                                ins = mm(o, w[:, k, half * P:(half + 1) * P], arena[:, Y_TILE[k], 0:n],
                                         start=k == BRANCH[b][0], stop=k == BRANCH[b][-1])
                            ins.then_inc(branch_done, 1)

            def out_proj(l):
                pe.wait_ge(m_ready, 8 * (l + 1))
                for c in range(4):
                    landed(pe, ("wo", l, c))
                    w = chunk(("wo", l, c))
                    for tt in range(QT[l]):
                        r = c * QT[l] + tt
                        if r >= 8:
                            pe.wait_ge(upd_ready, 4 * QT0[l] + r - 7)
                        for k in range(KD):
                            ins = mm(banks[:, r % 8, 0:CW], mT[:, k, tt * P:(tt + 1) * P], w[:, k, :],
                                     start=k == 0, stop=k == KD - 1)
                        ins.then_inc(wo_done, 1)

            def route(l):
                pe.wait_ge(small_in[l], SMALL)
                for tt in range(QT[l]):
                    for k in range(KD):
                        ins = mm(banks[:, 0, tt * NR:(tt + 1) * NR], hT[:, k, tt * P:(tt + 1) * P], w_router[:, k, :],
                                 start=k == 0, stop=k == KD - 1)
                ins.then_inc(lg_done, 1)

            def ranks(l):
                pe.wait_ge(pick_ready, l + 1)
                for tt in range(QT[l]):
                    for u in range(tt + 1):
                        mm(banks[:, 1, tt * NE:(tt + 1) * NE], C["upper"] if u == tt else C["ones"], both[:, u, :],
                           start=u == 0, stop=u == tt)
                for u in range(QT[l]):
                    ins = mm(banks[:, 1, 4 * NE:5 * NE], C["ones"], both[:, u, :], start=u == 0, stop=u == QT[l] - 1)
                ins.then_inc(rank_done, 1)

            def hold():
                pe.nop().then_inc(pe_held, 1)

            def turn_x(b):
                for k in range(KD):
                    ins = turn(banks[:, 0, k * CAP:(k + 1) * CAP], xe[b][:, k::KD], ident[0:CAP, 0:CAP])
                return ins

            def gate_up(b, w, o):
                for k in range(KD):
                    ins = mm(banks[0:CAP, o, 0:DE], xeT[b][:, k, :], w[:, k * DE:(k + 1) * DE],
                             start=k == 0, stop=k == KD - 1)
                return ins

            def turn_hid():
                for k in range(2):
                    ins = turn(banks[:, 1, k * CAP:(k + 1) * CAP], hid[:, k::2], ident[0:CAP, 0:CAP])
                return ins

            def down(w):
                for half in range(2):
                    for k in range(2):
                        ins = mm(banks[0:CAP, 4 + half, :], hidT[:, k, :], w[:, k * D + half * 512:k * D + half * 512 + 512],
                                 start=k == 0, stop=k == 1)
                return ins

            def slot_of(key):
                return ring[:, AT[key] % SLOTS, :]

            def step_x(l, e, i=None):
                n = E0[l] + e
                pe.wait_ge(xe_in[n % 3], lin(i, 16 * (n // 3 + 1), 16))
                if n:
                    pe.wait_ge(xeT_ready, lin(i, n, UNROLL))
                hold()
                turn_x(n % 3).then_inc(xe_turned, 1)

            def step_gu(l, e, i=None):
                n = E0[l] + e
                landed(pe, ("eg", l, e), i)
                if n:
                    pe.wait_ge(hid_ready, lin(i, n, UNROLL))
                pe.wait_ge(xeT_ready, lin(i, n + 1, UNROLL))
                gate_up(n % 3, slot_of(("eg", l, e)), 2).then_inc(e_gate_done, 1)
                landed(pe, ("eu", l, e), i)
                gate_up(n % 3, slot_of(("eu", l, e)), 3).then_inc(e_up_done, 1)

            def step_h(l, e, i=None):
                n = E0[l] + e
                if n:
                    pe.wait_ge(hidT_ready, lin(i, n, UNROLL))
                pe.wait_ge(hid_ready, lin(i, n + 1, UNROLL))
                hold()
                turn_hid().then_inc(hid_turned, 1)

            def step_d(l, e, i=None):
                n = E0[l] + e
                landed(pe, ("ed", l, e), i)
                if n:
                    pe.wait_ge(y_out, lin(i, n, UNROLL))
                pe.wait_ge(hidT_ready, lin(i, n + 1, UNROLL))
                down(slot_of(("ed", l, e))).then_inc(down_done, 1)

            def expert_step(l, e, i=None):
                step_h(l, e, i)
                if e + 2 < NE:
                    step_x(l, e + 2, i)
                if e + 1 < NE:
                    step_gu(l, e + 1, i)
                step_d(l, e, i)

            def experts(l):
                pe.wait_ge(mod_out, 36 if l == 0 else 48)
                step_x(l, 0)
                step_x(l, 1)
                step_gu(l, 0)
                for e in range(3):
                    expert_step(l, e)
                with pe.Fori(0, 9) as i:
                    for e in range(3, 6):
                        expert_step(l, e, i)
                for e in range(30, NE):
                    expert_step(l, e)

            def spill(l):
                pe.wait_ge(slots_ready, l + 1)
                pe.wait_ge(y_out, E0[l] + NE)
                n_spill = pe.value_load(meta[0:1, 0:1], min_val=0, max_val=SPILL[l])
                with pe.If(n_spill > 0):
                    with pe.Fori(0, SPILL[l]) as b:
                        with pe.If(b < n_spill):
                            step = spill_step[l]
                            pe.wait_ge(spill_dma[l], b * 64 + 64)
                            hold()
                            turn_x(0).then_inc(step, 1)
                            pe.wait_ge(step, b * 9 + 3)
                            gate_up(0, spill_gu[0], 2)
                            gate_up(0, spill_gu[1], 3).then_inc(step, 1)
                            pe.wait_ge(step, b * 9 + 6)
                            hold()
                            turn_hid().then_inc(step, 1)
                            pe.wait_ge(step, b * 9 + 8)
                            down(spill_d).then_inc(step, 1)
                    pe.wait_ge(step, n_spill * 9 + 1)
                    hold()

            for l in range(DEPTH):
                if l == 0:
                    for c in range(12):
                        mod(0, c)
                norm_turn(2 * l)
                project(l)
                attention(l)
                merge(l)
                out_proj(l)
                pe.wait_ge(upd_ready, 4 * (QT0[l] + QT[l]))
                for c in range(12, 24):
                    mod(l, c)
                norm_turn(2 * l + 1)
                route(l)
                if l == 0:
                    for c in range(4):
                        mod(1, c)
                ranks(l)
                if l == 0:
                    for c in range(4, 12):
                        mod(1, c)
                experts(l)
                spill(l)

        @block.scalar
        def _(act):
            seq = [0]
            fn = nc.scalar.activation

            def link(ins):
                seq[0] += 1
                ins.then_inc(act_seq, 1)
                act.wait_ge(act_seq, seq[0])

            def small_loads(l):
                for dst, src in (
                    (sinks_bc[:, :], t["sinks"][l].partition_broadcast(P)),
                    (convw[:, :, :], t["conv_w"][l].rearrange("(c p) j -> p c j", p=P)),
                    (w_router[:, :, 0:NG], t["w_rg"][l].rearrange("(p k) n -> p k n", k=KD)),
                    (w_router[:, :, NG:NR], t["w_re"][l].rearrange("(p k) n -> p k n", k=KD)),
                    (b_router[:, 0:NG], t["b_rg"][l].partition_broadcast(P)),
                    (b_router[:, NG:NR], t["b_re"][l].partition_broadcast(P)),
                ):
                    act.dma_start(dst, src).then_inc(small_in[l], 16)

            def load_g(m):
                src = [t["g_attn"][0], t["g_ffn"][0], t["g_attn"][1], t["g_ffn"][1], t["g_final"]][m]
                act.dma_start(g_bc, src.partition_broadcast(P)).then_inc(g_in, 16)

            def load_rev(l):
                for r in range(2):
                    for h in range(H_NA):
                        off = ((l * H_NA + h) * RPB_R + 5 - r) * RPB_C - 48
                        src = bass.AP(t["rpb"].tensor, off, [[1, GRID_W], [RPB_C, 6], [1, GRID_W]])
                        dst = rev[r * GRID_W:(r + 1) * GRID_W, h * 384:(h + 1) * 384]
                        act.dma_start(dst.rearrange("p (j c) -> p j c", j=6), src).then_inc(rev_in, 16)

            act.dma_start(cond[:, 0, :], t["c"][0].rearrange("(p k) -> p k", k=KD)).then_inc(cond_in, 16)
            act.dma_start(cond[:, 1, :], t["c_ctx"].rearrange("(p k) -> p k", k=KD)).then_inc(cond_in, 16)
            def load_bias(l, sec):
                act.dma_start(modc[:, sec % 3, :], t["b_mod"][l][sec * D:(sec + 1) * D].partition_broadcast(P))\
                   .then_inc(bias_in[sec % 3], 16)

            load_bias(0, 0)
            act.wait_ge(cond_in, 32)
            fn(cond_s[:, :, :], cond[:, :, :], ACT.Silu).then_inc(cond_act, 1)
            act.wait_ge(mod_done, 1)
            load_bias(0, 1)
            act.wait_ge(mod_done, 2)
            act.dma_start(X[:, 0:2, :], t["x"][0].rearrange("(t p) d -> p t d", p=P)).then_inc(x_in, 16)
            act.wait_ge(mod_done, 4)
            act.dma_start(X[:, 2:4, :], t["ctx"][0].rearrange("(t p) d -> p t d", p=P)).then_inc(x_in, 16)
            load_g(0)
            act.wait_ge(mod_done, 6)
            load_bias(0, 2)
            act.dma_start(consts[:, :], t["consts"]).then_inc(consts_in, 16)
            small_loads(0)
            load_rev(0)

            def spread(dst, section, s):
                for half in range(2):
                    ins = fn(dst[64 * half:64 * half + 64, :], modc[64 * s:64 * s + 64, section, :], ACT.Copy)
                return ins

            def streams(m):
                return 1 if m == 3 else 2

            def norm(m):
                l, ffn = divmod(m, 2)
                if m >= 1:
                    act.wait_ge(scale_ready, m)
                    if ffn:
                        act.wait_ge(s_dve, lat_steps(l, len(STEPS[l]) - 1))
                    load_g(m)
                for n, tt in enumerate(NORM_TILES[m]):
                    if m == 0:
                        act.wait_ge(x_in, 32)
                    elif ffn:
                        act.wait_ge(x_attn, 4 * QT0[l] + 3 * QT[l] + tt + 1)
                        if n == 0:
                            act.wait_ge(wo_done, 4 * (QT0[l] + QT[l]))
                    else:
                        act.wait_ge(x_moe, tt + 1)
                    ins = fn(htok[:, tt, :], X[:, tt, :], ACT.Square, accum_out=stat[:, tt:tt + 1])
                    ins.then_inc(sq_done, 1)
                if m == 2:
                    load_rev(1)
                act.wait_ge(ms_ready, m + 1)
                fn(stat[:, 8:12], stat[:, 4:8], ACT.Sqrt).then_inc(std_ready, 1)
                act.wait_ge(mod_out, 12 * m + 4)
                if ffn:
                    act.wait_ge(upd_ready, 4 * (QT0[l] + QT[l]))
                for s in range(streams(m)):
                    ins = spread(mod_shift[s], 0, s)
                ins.then_inc(shift_ready, 1)
                for n, tt in enumerate(NORM_TILES[m]):
                    act.wait_ge(h_turned, 2 * (N0[m] + n) + 1)
                    fn(hT[:, 0:4, tt * P:(tt + 1) * P],
                       banks[:, 2 * n, :].rearrange("p (k s) -> p k s", k=4), ACT.Copy).then_inc(hT_act, 1)

            def project(l):
                for o, (what, c, arg) in enumerate(OUTS[l]):
                    if by_act(o):
                        act.wait_ge(proj_done, l * N_OUT + o + 1)
                        dst, n = out_place(l, what, c, arg)
                        fn(dst, banks[:, o % 8, 0:n], ACT.Copy).then_inc(out_act, 1)

            def attention(l):
                n = len(STEPS[l])
                for s in range(n + 3):
                    g = STEP0[l] + s
                    if 0 <= s - 1 < n:
                        b = (s - 1) % 3
                        act.wait_ge(max_ready, g)
                        w = width(l, s - 1)
                        for q in range(2):
                            ins = fn(S[b][:, q, 0:w], S[b][:, q, 0:w], ACT.Exp, bias=negmax[:, b, q:q + 1],
                                     accum_out=esum[:, b, q:q + 1])
                        ins.then_inc(exp_done, 1)
                    if 0 <= s - 2 < n:
                        k = 2 if STEPS[l][s - 2][2] else 4
                        act.wait_ge(p_turned, g - 1)
                        if g - 2 > 0:
                            act.wait_ge(pv_done, g - 2)
                        fn(PT[:, 0:k, P:2 * P], banks[:, 5, 0:k * P].rearrange("p (k q) -> p k q", k=k), ACT.Copy)\
                            .then_inc(pt_act, 1)
                    if s < n:
                        on_ctx = STEPS[l][s][2]
                        act.wait_ge(sc_done, g + 1)
                        if g >= 3:
                            act.wait_ge(p_turned, g - 2)
                        k0 = 0 if on_ctx else SEQ
                        fn(S[s % 3][:, :, k0:k0 + CTX], banks[:, 2 * (s % 2) + 1, :].rearrange("p (b k) -> p b k", b=2), ACT.Copy,
                           scale=SCALE).then_inc(s_act, 1)
                    if 0 <= s - 3 < n:
                        family, h, on_ctx = STEPS[l][s - 3]
                        tn, p0 = (T_NQ + h // 2, HD * (h % 2)) if family == "na" else (T_WQ + h % 3, HD * (h // 3))
                        q0 = SEQ if on_ctx else 0
                        act.wait_ge(pv_done, g - 2)
                        fn(arena[p0:p0 + HD, tn, q0:q0 + 2 * P], banks[0:HD, 6 + (s - 3) % 2, 0:2 * P], ACT.Copy)\
                            .then_inc(o_ready, 1)

            def gates(l):
                n = QN[l]
                for pair in range(4):
                    for r in range(6):
                        act.wait_ge(gate_done, 24 * l + 6 * pair + r + 1)
                        if pair:
                            act.wait_ge(m_ready, 8 * l + 2 * (pair - 1) + r % 2 + 1)
                        fn(sig[r][:, 0:n], banks[:, (12 * pair + r) % 8, 0:n], ACT.Sigmoid).then_inc(sig_ready, 1)
                act.wait_ge(branch_done, 24 * (l + 1))
                for s in range(2 - l):
                    ins = spread(gate_bc[s], 2, s)
                ins.then_inc(gate_ready, 1)
                act.wait_ge(gate_ready, l + 1)
                for sec in range(3, 6):
                    load_bias(l, sec)

            def route(l):
                nt = QT[l]
                act.wait_ge(mod_out, 24 * (l + 1))
                for s in range(2 - l):
                    ins = spread(gate_f[s], 2, s)
                ins.then_inc(gate_f_ready, 1)
                if l == 0:
                    act.wait_ge(gate_f_ready, 1)
                    for sec in range(3):
                        load_bias(1, sec)
                for r, (dst, src) in enumerate((
                    (prod[:, 0, 0:nt, 0:8], prod[:, 0, 0:nt, 0:8]),
                    (rt[:, 16:16 + nt], rt[:, 12:12 + nt]),
                )):
                    act.wait_ge(router_exp_in, 2 * l + r + 1)
                    fn(dst, src, ACT.Exp).then_inc(router_exp, 1)

            def silu(l, e, i=None):
                n = E0[l] + e
                if n:
                    act.wait_ge(hid_ready, lin(i, n, UNROLL))
                act.wait_ge(e_gate_done, lin(i, n + 1, UNROLL))
                fn(act_g, banks[0:CAP, 2, 0:DE], ACT.Silu).then_inc(silu_ready, 1)

            def store_y(l, e, i=None):
                n = E0[l] + e
                row = e * CAP if i is None else act.snap(i * (UNROLL * CAP) + e * CAP)
                row2 = (e + 5) * CAP if i is None else act.snap(i * (UNROLL * CAP) + (e + 5) * CAP)
                if n:
                    act.wait_ge(y_stored, lin(i, 16 * n, 16 * UNROLL))
                act.wait_ge(down_done, lin(i, n + 1, UNROLL))
                fn(y_sb, banks[0:CAP, 4:6, :].rearrange("p a b -> p (a b)"), ACT.Copy).then_inc(y_out, 1)
                act.wait_ge(y_out, lin(i, n + 1, UNROLL))
                act.dma_start(yd[bass.ds(row, CAP), :], y_sb).then_inc(y_stored, 16)
                if e + 5 < NE:
                    act.wait_ge(xe_turned, lin(i, n + 3, UNROLL))
                    act.dma_start(xe[(n + 5) % 3], xd[bass.ds(row2, CAP), :]).then_inc(xe_in[(n + 5) % 3], 16)

            def experts(l):
                act.wait_ge(xd_zero, ZEROED)
                act.wait_ge(scattered, 32 * (QT0[l] + QT[l]))
                for e in range(5 - 2):
                    n = E0[l] + e
                    act.dma_start(xe[n % 3], xd[e * CAP:(e + 1) * CAP, :]).then_inc(xe_in[n % 3], 16)
                if l == 0:
                    small_loads(1)
                for e in (3, 4):
                    n = E0[l] + e
                    act.wait_ge(xe_turned, n - 2)
                    act.dma_start(xe[n % 3], xd[e * CAP:(e + 1) * CAP, :]).then_inc(xe_in[n % 3], 16)
                silu(l, 0)
                for e in range(3):
                    silu(l, e + 1)
                    store_y(l, e)
                with act.Fori(0, 8) as i:
                    for e in range(3, 6):
                        silu(l, e + 1, i)
                        store_y(l, e, i)
                for e in range(27, NE):
                    if e + 1 < NE:
                        silu(l, e + 1)
                    store_y(l, e)

            def spill(l):
                act.wait_ge(slots_ready, l + 1)
                act.wait_ge(y_stored, 16 * (E0[l] + NE))
                n_spill = act.value_load(meta[0:1, 0:1], min_val=0, max_val=SPILL[l])
                step = spill_step[l]
                with act.If(n_spill > 0):
                    act.wait_ge(xe_turned, E0[l] + NE)
                    act.nop().then_inc(step, 1)
                    act.nop().then_inc(spill_out[l], 16)
                    with act.Fori(0, SPILL[l]) as b:
                        with act.If(b < n_spill):
                            row = act.snap(b * CAP + MAIN)
                            act.wait_ge(step, b * 9 + 1)
                            act.dma_start(xe[0], xd[bass.ds(row, CAP), :]).then_inc(spill_dma[l], 16)
                            act.wait_ge(step, b * 9 + 4)
                            fn(act_g, banks[0:CAP, 2, 0:DE], ACT.Silu).then_inc(step, 1)
                            act.wait_ge(spill_out[l], b * 16 + 16)
                            act.wait_ge(step, b * 9 + 9)
                            fn(y_sb, banks[0:CAP, 4:6, :].rearrange("p a b -> p (a b)"), ACT.Copy).then_inc(step, 1)
                            act.wait_ge(step, b * 9 + 10)
                            act.dma_start(yd[bass.ds(row, CAP), :], y_sb).then_inc(spill_out[l], 16)
                    act.wait_ge(spill_out[l], n_spill * 16 + 16)
                    act.nop().then_inc(step, 1)
                act.nop().then_inc(rows_done, 1)

            for l in range(DEPTH):
                norm(2 * l)
                project(l)
                attention(l)
                gates(l)
                norm(2 * l + 1)
                route(l)
                experts(l)
                spill(l)

            act.wait_ge(scale_ready, 4)
            load_g(4)
            for tt in range(2):
                act.wait_ge(x_moe, QT0[1] + tt + 1)
                fn(htok[:, tt, :], X[:, tt, :], ACT.Square, accum_out=stat[:, tt:tt + 1]).then_inc(sq_done, 1)
            act.wait_ge(ms_ready, 5)
            fn(stat[:, 8:12], stat[:, 4:8], ACT.Sqrt).then_inc(std_ready, 1)
            for tt in range(2):
                act.wait_ge(fin_ready, tt + 1)
                act.dma_start(out[0, tt * P:(tt + 1) * P, :], htok[:, tt, :]).then_inc(stored, 16)
            act.wait_ge(stored, 32)

        @block.vector
        def _(dve):
            v = nc.vector
            seq = [0]

            def link(ins):
                seq[0] += 1
                ins.then_inc(dve_seq, 1)
                dve.wait_ge(dve_seq, seq[0])

            dve.wait_ge(cond_act, 1)
            for s in range(2):
                v.tensor_copy(cond_bc[:, :, 64 * s:64 * s + 64],
                              cond_s[:, s, :].unsqueeze(2).to_broadcast([P, KD, 64])).then_inc(cond_ready, 1)

            def mod_add(l, c):
                m = 24 * l + c
                sec, q = divmod(c, 4)
                if q == 0:
                    dve.wait_ge(bias_in[sec % 3], 16 * (2 * l + c // 12 + 1))
                dve.wait_ge(mod_done, m + 1)
                dst = modc[:, sec % 3, q * CW:(q + 1) * CW]
                v.tensor_tensor(dst, banks[:, 4 + c % 4, 0:CW], dst, ALU.add).then_inc(mod_out, 1)

            def rstd(m, tiles):
                dve.wait_ge(sq_done, N0[m] + len(tiles))
                v.tensor_scalar(stat[:, 4:8], stat[:, 0:4], 1.0 / D, EPS, ALU.mult, ALU.add).then_inc(ms_ready, 1)
                dve.wait_ge(std_ready, m + 1)
                link(v.reciprocal(stat[:, 12:16], stat[:, 8:12]))

            def norm(m):
                l, ffn = divmod(m, 2)
                sec = 1
                dve.wait_ge(g_in, 16 * (m + 1))
                dve.wait_ge(mod_out, 12 * (m + 1))
                ins = v.scalar_tensor_tensor(modc[:, sec, :], modc[:, sec, :], 1.0, g_bc, ALU.add, ALU.mult)
                ins.then_inc(scale_ready, 1)
                dve.wait_ge(scale_ready, m + 1)
                if ffn:
                    dve.wait_ge(xd_zero, ZEROED)
                    dve.wait_ge(branch_done, 24 * (l + 1))
                    dve.wait_ge(upd_ready, 4 * (QT0[l] + QT[l]))
                for s in range(1 if m == 3 else 2):
                    for half in range(2):
                        link(v.tensor_copy(mod_scale[s][64 * half:64 * half + 64, :], modc[64 * s:64 * s + 64, sec, :]))
                for n, tt in enumerate(NORM_TILES[m]):
                    v.scalar_tensor_tensor(htok[:, tt, :], X[:, tt, :], stat[:, 12 + tt:13 + tt], mod_scale[tt // 2],
                                           ALU.mult, ALU.mult).then_inc(h_scaled, 1)
                for n, tt in enumerate(NORM_TILES[m]):
                    dve.wait_ge(h_turned, 2 * (N0[m] + n) + 2)
                    v.tensor_copy(hT[:, 4:8, tt * P:(tt + 1) * P],
                                  banks[:, 2 * n + 1, :].rearrange("p (k s) -> p k s", k=4)).then_inc(hT_dve, 1)

            def project(l):
                for o, (what, c, arg) in enumerate(OUTS[l]):
                    if by_act(o):
                        continue
                    dve.wait_ge(proj_done, l * N_OUT + o + 1)
                    if what == "bias":
                        v.tensor_tensor(strip[:, c, :].rearrange("p (j c) -> p j c", j=6),
                                        banks[:, o % 8, 0:384].rearrange("p (j c) -> p j c", j=6),
                                        C["mask_na"].unsqueeze(1).to_broadcast([P, 6, GRID_W]), ALU.add)\
                            .then_inc(out_dve, 1)
                    else:
                        dst, n = out_place(l, what, c, arg)
                        v.tensor_copy(dst, banks[:, o % 8, 0:n]).then_inc(out_dve, 1)
                ns = 2 - l
                for c in range(2):
                    dve.wait_ge(z_ready, 2 * l + c + 1)
                    z, a = (arena[:, q + c, 0:256 * ns].rearrange("p (s n) -> p s n", s=ns) for q in (T_AH, T_AC))
                    link(v.scalar_tensor_tensor(a[:, :, 1:256], z[:, :, 0:255], convw[:, c, 0:1], a[:, :, 1:256],
                                                ALU.mult, ALU.add))
                    v.scalar_tensor_tensor(a[:, :, 0:255], z[:, :, 1:256], convw[:, c, 2:3], a[:, :, 0:255],
                                           ALU.mult, ALU.add).then_inc(conv_done, 1)
                for r, tn in enumerate((T_WQ, T_WQ + 1, T_WQ + 2, T_WK)):
                    x = arena[:, tn, 0:SEQ]
                    dve.wait_ge(rope_mm, 4 * l + r + 1)
                    link(v.tensor_tensor(rope_t[:, r, :], x, C["cos"], ALU.mult))
                    link(v.tensor_tensor(x, banks[:, 4 + r, 0:SEQ], C["sin"], ALU.mult))
                    v.tensor_tensor(x, x, rope_t[:, r, :], ALU.add).then_inc(rope_done, 1)

            def attention(l):
                n = len(STEPS[l])
                for s in range(n + 2):
                    g = STEP0[l] + s
                    if 0 <= s - 2 < n:
                        k = 2 if STEPS[l][s - 2][2] else 4
                        dve.wait_ge(p_turned, g - 1)
                        if g - 2 > 0:
                            dve.wait_ge(pv_done, g - 2)
                        v.tensor_copy(PT[:, 0:k, 0:P], banks[:, 4, 0:k * P].rearrange("p (k q) -> p k q", k=k))\
                            .then_inc(pt_dve, 1)
                    if s < n:
                        family, h, on_ctx = STEPS[l][s]
                        buf = S[s % 3]
                        w = width(l, s)
                        if g >= 3:
                            dve.wait_ge(p_turned, g - 2)
                        if not on_ctx:
                            dve.wait_ge(sc_done, g + 1)
                            for b in range(2):
                                if family == "na":
                                    add = strip[:, h, (2 - 2 * b) * GRID_W:(6 - 2 * b) * GRID_W]
                                else:
                                    add = C["mask_win"][:, b * SEQ:(b + 1) * SEQ]
                                ins = v.scalar_tensor_tensor(buf[:, b, 0:SEQ], banks[:, 2 * (s % 2), b * SEQ:(b + 1) * SEQ],
                                                             SCALE, add, ALU.mult, ALU.add)
                            ins.then_inc(s_dve, 1)
                        if family == "win":
                            link(v.tensor_copy(buf[:, :, w - 1:w],
                                               sinks_bc[:, h:h + 1].unsqueeze(1).to_broadcast([P, 2, 1])))
                        dve.wait_ge(s_act, g + 1)
                        if not on_ctx:
                            dve.wait_ge(s_dve, lat_steps(l, s))
                        v.tensor_reduce(negmax[:, s % 3, :], buf[:, :, 0:w], AX.X, ALU.max, negate=True)\
                            .then_inc(max_ready, 1)
                    if 0 <= s - 1 < n:
                        b = (s - 1) % 3
                        k = width(l, s - 1) - (STEPS[l][s - 1][0] == "win")
                        dve.wait_ge(exp_done, g)
                        link(v.reciprocal(rsum[:, b, :], esum[:, b, :]))
                        for q in range(2):
                            ins = v.tensor_scalar(S[b][:, q, 0:k], S[b][:, q, 0:k], rsum[:, b, q:q + 1], None, ALU.mult)
                        ins.then_inc(p_ready, 1)

            def gates(l):
                n = QN[l]
                for pair in range(4):
                    for half in range(2):
                        for b in range(3):
                            dve.wait_ge(branch_done, 24 * l + 6 * pair + 3 * half + b + 1)
                            dve.wait_ge(sig_ready, 24 * l + 6 * pair + 2 * b + half + 1)
                            s = sig[2 * b + half][:, 0:n]
                            v.tensor_tensor(s, s, banks[:, (12 * pair + 6 + 3 * half + b) % 8, 0:n], ALU.mult)\
                                .then_inc(gated, 1)

            def residual(l):
                dve.wait_ge(gate_ready, l + 1)
                for c in range(4):
                    for tt in range(QT[l]):
                        r = c * QT[l] + tt
                        dve.wait_ge(wo_done, 4 * QT0[l] + r + 1)
                        if r >= 4:
                            dve.wait_ge(x_attn, 4 * QT0[l] + r - 3)
                        v.tensor_tensor(upd[r % 4], banks[:, r % 8, 0:CW], gate_bc[tt // 2][:, c * CW:(c + 1) * CW],
                                        ALU.mult).then_inc(upd_ready, 1)

            def route(l):
                nt = QT[l]
                dve.wait_ge(lg_done, l + 1)
                link(v.memset(g8[:, :, :], NEG))
                link(v.tensor_tensor(lg[:, 0:nt, :], banks[:, 0, 0:nt * NR].rearrange("p (t n) -> p t n", t=nt),
                                     b_router[:, :].unsqueeze(1).to_broadcast([P, nt, NR]), ALU.add))
                link(v.tensor_copy(g8[:, 0:nt, 0:NG], lg[:, 0:nt, 0:NG]))
                for tt in range(nt):
                    ins = v.max(top_g[:, tt, :], g8[:, tt, :])
                link(ins)
                for tt in range(nt):
                    v.max_index(idx_g[:, tt, :], top_g[:, tt, :], g8[:, tt, :])
                v.tensor_tensor(prod[:, 0, 0:nt, 0:8], g8[:, 0:nt, :], top_g[:, 0:nt, 0:1].to_broadcast([P, nt, 8]),
                                ALU.subtract).then_inc(router_exp_in, 1)
                dve.wait_ge(router_exp_in, 2 * l + 1)
                link(v.tensor_copy(rt[:, 0:nt], idx_g[:, 0:nt, 0]))
                oh = cnt[:, 0:4 * nt].rearrange("p (t g) -> p t g", g=NG)
                pen = cnt[:, 16:16 + 4 * nt].rearrange("p (t g) -> p t g", g=NG)
                link(v.tensor_tensor(oh, C["iota"][:, 0:NG].unsqueeze(1).to_broadcast([P, nt, NG]),
                                     rt[:, 0:nt].unsqueeze(2).to_broadcast([P, nt, NG]), ALU.is_equal))
                link(v.tensor_scalar(pen, oh, -1.0, -NEG, ALU.add, ALU.mult))
                le4 = lem[:, 0:nt, :].rearrange("p t (g e) -> p t g e", g=NG)
                link(v.tensor_tensor(le4, lg[:, 0:nt, NG:NR].rearrange("p t (g e) -> p t g e", g=NG),
                                     oh.unsqueeze(3).to_broadcast([P, nt, NG, EPG]), ALU.mult))
                link(v.tensor_tensor(le4, le4, pen.unsqueeze(3).to_broadcast([P, nt, NG, EPG]), ALU.add))
                for tt in range(nt):
                    ins = v.max(top_e[:, tt, :], lem[:, tt, :])
                link(ins)
                for tt in range(nt):
                    ins = v.max_index(idx_e[:, tt, :], top_e[:, tt, :], lem[:, tt, :])
                link(ins)
                ef = slots_f
                link(v.tensor_copy(ef[:, :, 0:nt], idx_e[:, 0:nt, 0:2].rearrange("p t c -> p c t")))
                for c in range(2):
                    ins = v.tensor_tensor(pick[:, c, 0:nt, :], C["iota"].unsqueeze(1).to_broadcast([P, nt, NE]),
                                          ef[:, c, 0:nt].unsqueeze(2).to_broadcast([P, nt, NE]), ALU.is_equal)
                link(ins)
                v.tensor_tensor(both[:, 0:nt, :], pick[:, 0, 0:nt, :], pick[:, 1, 0:nt, :], ALU.add)\
                    .then_inc(pick_ready, 1)
                v.tensor_tensor(rt[:, 12:12 + nt], top_e[:, 0:nt, 1], top_e[:, 0:nt, 0], ALU.subtract)\
                    .then_inc(router_exp_in, 1)

            def weights(l):
                nt = QT[l]
                dve.wait_ge(router_exp, 2 * l + 2)
                link(v.tensor_reduce(rt[:, 4:4 + nt], prod[:, 0, 0:nt, 0:8], AX.X, ALU.add))
                link(v.tensor_scalar(rt[:, 20:20 + nt], rt[:, 16:16 + nt], 1.0, None, ALU.add))
                link(v.tensor_tensor(rt[:, 24:24 + nt], rt[:, 20:20 + nt], rt[:, 4:4 + nt], ALU.mult))
                link(v.reciprocal(wts[:, 0, 0:nt], rt[:, 24:24 + nt]))
                v.tensor_tensor(wts[:, 1, 0:nt], wts[:, 0, 0:nt], rt[:, 16:16 + nt], ALU.mult).then_inc(wts_ready, 1)

            def place(l):
                nt = QT[l]
                dve.wait_ge(rank_done, l + 1)
                v.tensor_copy(rank[:, 0:nt, :], banks[:, 1, 0:nt * NE].rearrange("p (t e) -> p t e", t=nt))
                link(v.tensor_copy(cnt[:, 0:NE], banks[:, 1, 4 * NE:5 * NE]))

                def picked(dst, table):
                    link(v.tensor_tensor(prod[:, 0, 0:nt, :], pick[:, 0, 0:nt, :], table, ALU.mult))
                    link(v.tensor_tensor(prod[:, 1, 0:nt, :], pick[:, 1, 0:nt, :], table, ALU.mult))
                    link(v.tensor_reduce(dst, prod[:, :, 0:nt, :], AX.X, ALU.add))

                def small(n):
                    return rt[:, n:n + 2 * nt].rearrange("p (c t) -> p c t", c=2)

                rr, s0, s1 = small(32), small(40), small(48)
                picked(rr, rank[:, 0:nt, :])
                picked(s0, C["slot0"].unsqueeze(1).to_broadcast([P, nt, NE]))
                over = prod[:, :, :, :].rearrange("p a b c -> p (a b c)")[:, 0:NE * (NBK - 1)]\
                    .rearrange("p (e m) -> p e m", e=NE)
                link(v.tensor_tensor(over, cnt[:, 0:NE].unsqueeze(2).to_broadcast([P, NE, NBK - 1]),
                                     C["thr"].unsqueeze(1).to_broadcast([P, NE, NBK - 1]), ALU.is_gt))
                nx, xin, alt = (cnt[:, q * NE:(q + 1) * NE] for q in (1, 2, 3))
                link(v.tensor_reduce(nx, over, AX.X, ALU.add))
                link(v.tensor_tensor_scan(xin, C["ones"][:, 0:NE], nx, 0.0, ALU.mult, ALU.add))
                link(v.tensor_tensor(alt, xin, nx, ALU.subtract))
                link(v.tensor_scalar(alt, alt, float(CAP), float(MAIN - CAP), ALU.mult, ALU.add))
                link(v.tensor_tensor(alt, alt, C["slot0"], ALU.subtract))
                picked(s1, alt.unsqueeze(1).to_broadcast([P, nt, NE]))
                ge = rt[:, 56:56 + 2 * nt].rearrange("p (c t) -> p c t", c=2)
                link(v.tensor_scalar(ge, rr, float(CAP), None, ALU.is_ge))
                link(v.tensor_tensor(s1, s1, ge, ALU.mult))
                link(v.tensor_tensor(s0, s0, rr, ALU.add))
                link(v.tensor_tensor(slots_f[:, :, 0:nt], s0, s1, ALU.add))
                link(v.tensor_copy(slots_u[:, :, 0:nt], slots_f[:, :, 0:nt]))
                nb = SPILL[0]
                cmp = prod[0:1, :, :, :].rearrange("p a b c -> p (a b c)")
                own = rank[0:1, :, :].rearrange("p a b -> p (a b)")
                for half in range(2):
                    hb = nb // 2
                    cc = cmp[:, 0:hb * NE].rearrange("p (b e) -> p b e", b=hb)
                    link(v.tensor_tensor(cc, xin[0:1, :].unsqueeze(1).to_broadcast([1, hb, NE]),
                                         C["iota"][0:1, half * hb:(half + 1) * hb].unsqueeze(2).to_broadcast([1, hb, NE]),
                                         ALU.is_le))
                    link(v.tensor_reduce(own[:, 1 + half * hb:1 + (half + 1) * hb], cc, AX.X, ALU.add))
                link(v.tensor_scalar(own[:, 1:1 + nb], own[:, 1:1 + nb], float(NE - 1), None, ALU.min))
                link(v.tensor_copy(own[:, 0:1], xin[0:1, NE - 1:NE]))
                v.tensor_copy(meta[:, :], own[:, 0:1 + nb]).then_inc(slots_ready, 1)

            def take_xT(l, e, i=None):
                n = E0[l] + e
                if n >= 3:
                    dve.wait_ge(e_up_done, lin(i, n - 2, UNROLL))
                dve.wait_ge(xe_turned, lin(i, n + 1, UNROLL))
                v.tensor_copy(xeT[n % 3], banks[:, 0, :].rearrange("p (k s) -> p k s", k=KD)).then_inc(xeT_ready, 1)

            def take_hid(l, e, i=None):
                n = E0[l] + e
                if n:
                    dve.wait_ge(hid_turned, lin(i, n, UNROLL))
                dve.wait_ge(silu_ready, lin(i, n + 1, UNROLL))
                dve.wait_ge(e_up_done, lin(i, n + 1, UNROLL))
                v.tensor_tensor(hid, act_g, banks[0:CAP, 3, 0:DE], ALU.mult).then_inc(hid_ready, 1)

            def take_hidT(l, e, i=None):
                n = E0[l] + e
                if n:
                    dve.wait_ge(down_done, lin(i, n, UNROLL))
                dve.wait_ge(hid_turned, lin(i, n + 1, UNROLL))
                v.tensor_copy(hidT[:, :, :], banks[:, 1, 0:2 * CAP].rearrange("p (k s) -> p k s", k=2))\
                    .then_inc(hidT_ready, 1)

            def expert_step(l, e, i=None):
                take_hidT(l, e, i)
                if e + 2 < NE:
                    take_xT(l, e + 2, i)
                if e + 1 < NE:
                    take_hid(l, e + 1, i)

            def experts(l):
                take_xT(l, 0)
                take_xT(l, 1)
                take_hid(l, 0)
                for e in range(3):
                    expert_step(l, e)
                with dve.Fori(0, 9) as i:
                    for e in range(3, 6):
                        expert_step(l, e, i)
                for e in range(30, NE):
                    expert_step(l, e)

            def spill(l):
                n_spill = dve.value_load(meta[0:1, 0:1], min_val=0, max_val=SPILL[l])
                step = spill_step[l]
                with dve.If(n_spill > 0):
                    with dve.Fori(0, SPILL[l]) as b:
                        with dve.If(b < n_spill):
                            dve.wait_ge(step, b * 9 + 2)
                            v.tensor_copy(xeT[0], banks[:, 0, :].rearrange("p (k s) -> p k s", k=KD)).then_inc(step, 1)
                            dve.wait_ge(step, b * 9 + 5)
                            v.tensor_tensor(hid, act_g, banks[0:CAP, 3, 0:DE], ALU.mult).then_inc(step, 1)
                            dve.wait_ge(step, b * 9 + 7)
                            v.tensor_copy(hidT[:, :, :], banks[:, 1, 0:2 * CAP].rearrange("p (k s) -> p k s", k=2))\
                                .then_inc(step, 1)

            def combine(l):
                dve.wait_ge(gate_f_ready, l + 1)
                dve.wait_ge(wts_ready, l + 1)
                for tt in range(QT[l]):
                    dve.wait_ge(got_in[tt % 2], 32 * (QT0[l] // 2 + tt // 2 + 1))
                    for c in range(2):
                        y = got[tt % 2][c]
                        ins = v.scalar_tensor_tensor(y, y, wts[:, c, tt:tt + 1], gate_f[tt // 2], ALU.mult, ALU.mult)
                    ins.then_inc(y_gated, 1)

            for l in range(DEPTH):
                if l == 0:
                    for c in range(12):
                        mod_add(0, c)
                rstd(2 * l, NORM_TILES[2 * l])
                norm(2 * l)
                project(l)
                attention(l)
                gates(l)
                residual(l)
                rstd(2 * l + 1, NORM_TILES[2 * l + 1])
                for c in range(12, 24):
                    mod_add(l, c)
                norm(2 * l + 1)
                route(l)
                if l == 0:
                    for c in range(4):
                        mod_add(1, c)
                weights(l)
                place(l)
                if l == 0:
                    for c in range(4, 12):
                        mod_add(1, c)
                experts(l)
                spill(l)
                combine(l)

            rstd(4, [0, 1])
            dve.wait_ge(g_in, 80)
            for tt in range(2):
                v.scalar_tensor_tensor(htok[:, tt, :], X[:, tt, :], stat[:, 12 + tt:13 + tt], g_bc,
                                       ALU.mult, ALU.mult).then_inc(fin_ready, 1)


INPUTS = ["x", "c", "ctx", "c_ctx", "w_mod", "b_mod", "g_attn", "g_ffn", "w_in", "conv_w", "rpb", "sinks",
          "w_branch", "w_o", "w_rg", "b_rg", "w_re", "b_re", "w_e_gate", "w_e_up", "w_e_down", "g_final"]


def kernel(**inputs):
    import concourse.bacc as bacc
    from concourse.bass_utils import run_bass_kernel_spmd

    nc = bacc.Bacc("TRN2", target_bir_lowering=False, num_devices=1)
    arrays, t = {}, {}
    given = {n: np.ascontiguousarray(inputs[n]) for n in INPUTS}
    given["conv_w"] = np.ascontiguousarray(given["conv_w"].transpose(0, 2, 1))
    given["consts"] = constants()
    for name, a in given.items():
        arrays[f"in_{name}"] = a
        t[name] = nc.dram_tensor(f"in_{name}", a.shape, mybir.dt.from_np(a.dtype), kind="ExternalInput").ap()
    out = nc.dram_tensor("out", (1, SEQ, D), F32, kind="ExternalOutput").ap()
    program(nc, t, out)
    return run_bass_kernel_spmd(nc, [arrays], core_ids=[0]).results[0]["out"]
```

```python
from contextlib import ExitStack

import numpy as np
import concourse.bass as bass
from concourse import mybir

P = 128
D = 1024
KD = D // P
SEQ, CTX, DEPTH = 256, 256, 2
NTOK = SEQ + CTX
GRID_W, HD, D_CONV, CONV_W = 64, 64, 256, 3
H_NA, WIN_R_MAX, WIN_C = 6, 8, 16
H_Q, H_KV, WINDOW = 6, 2, 128
D_NA, D_SW, D_KV = H_NA * HD, H_Q * HD, H_KV * HD
COL_NQ = 3 * D_CONV
COL_NV = COL_NQ + 2 * D_NA
COL_WQ = COL_NV + D_NA
COL_WK = COL_WQ + D_SW
COL_WV = COL_WK + D_KV
COL_G = COL_WV + D_KV
NG, EPG = 4, 8
NE = NG * EPG
NR = NG + NE
DE = 256
EPS = 1e-6
NEG = -1e30
ROPE_BASE = 10000.0
RPB_R, RPB_C = 2 * WIN_R_MAX - 1, 2 * WIN_C - 1
ROWS = SEQ // GRID_W
SCALE = HD ** -0.5

CW = 256
SLOTS = 6
UNROLL = 6
LOOPED = (NE - 8) // UNROLL
KU = 1
AHEAD = 4
CAP = 64
MAIN = NE * CAP
SPILL = [2 * NTOK // CAP, 2 * SEQ // CAP]
ROWS_D = MAIN + SPILL[0] * CAP
NBK = NTOK // CAP

F32 = mybir.dt.float32
F32R = mybir.dt.float32r
I32 = mybir.dt.int32
U32 = mybir.dt.uint32
ALU = mybir.AluOpType
ACT = mybir.ActivationFunctionType
AX = mybir.AxisListType

CONST_COLS = dict(ident=P, upper=P, ones=P, rot=P, flip=P, cos=SEQ, sin=SEQ, mask_na=GRID_W,
                  mask_win=2 * SEQ, iota=NE, slot0=NE, thr=NBK - 1)


def constants():
    p = np.arange(P)
    c = {"ident": np.eye(P), "ones": np.ones((P, P)),
         "upper": (p[:, None] < p[None, :]).astype(np.float32)}
    rot = np.zeros((P, P))
    for m in range(P):
        if m % 32 < 16:
            rot[m + 16, m] = -1.0
        else:
            rot[m - 16, m] = 1.0
    c["rot"] = rot
    flip = np.zeros((P, P))
    flip[(p // 64) * 64 + 63 - p % 64, p] = 1.0
    c["flip"] = flip
    t = np.arange(SEQ)
    quarter = HD // 4
    inv = np.float32(ROPE_BASE) ** (-np.arange(quarter, dtype=np.float32) / np.float32(quarter))
    pos = np.where((p % HD < HD // 2)[:, None], (t // GRID_W)[None], (t % GRID_W)[None])
    ang = pos.astype(np.float32) * inv[p % quarter][:, None].astype(np.float32)
    c["cos"], c["sin"] = np.cos(ang), np.sin(ang)
    col = p % GRID_W
    start = np.clip(col - WIN_C // 2, 0, GRID_W - WIN_C)
    kc = np.arange(GRID_W)[None]
    c["mask_na"] = np.where((kc >= start[:, None]) & (kc < start[:, None] + WIN_C), 0.0, NEG)
    k = np.arange(SEQ)[None]
    c["mask_win"] = np.concatenate(
        [np.where(np.abs(k - (b * P + p)[:, None]) <= WINDOW, 0.0, NEG) for b in range(2)], 1)
    c["iota"] = np.tile(np.arange(NE), (P, 1))
    c["slot0"] = np.tile(np.arange(NE) * CAP, (P, 1))
    c["thr"] = np.tile(np.arange(1, NBK) * CAP, (P, 1))
    return np.concatenate([c[n].astype(np.float32) for n in CONST_COLS], axis=1)


def weight_stream():
    out = []
    for l in range(DEPTH):
        if l == 0:
            out += [("mod", 0, c) for c in range(12)]
        out += [("in", l, c) for c in range(10)]
        for n in range(4):
            out += [("gate", l, 3 * n + b) for b in range(3)] + [("branch", l, n)]
        out += [("wo", l, c) for c in range(4)]
        if l == 0:
            out += [("mod", 0, c) for c in range(12, 24)] + [("mod", 1, c) for c in range(12)]
        out += [("eg", l, 0), ("eu", l, 0)]
        for e in range(NE):
            if e + 1 < NE:
                out += [("eg", l, e + 1), ("eu", l, e + 1)]
            out += [("ed", l, e)]
        if l == 0:
            out += [("mod", 1, c) for c in range(12, 24)]
    return out


PIECES = {("in", 7): 2, ("in", 8): 4, ("in", 9): 3}


def pieces(kind, index):
    if kind == "branch":
        return 3
    return PIECES.get((kind, index), 1)


STREAM = weight_stream()
AT = {key: j for j, key in enumerate(STREAM)}
LOADED = []
for _j, (_k, _l, _i) in enumerate(STREAM):
    LOADED.append((LOADED[_j - SLOTS] if _j >= SLOTS else 0) + 16 * pieces(_k, _i))


T_AH, T_AB, T_AC, T_NQ, T_WQ, T_NK, T_WK = 0, 2, 4, 6, 9, 12, 15
IN_TILES = {0: (0, 1), 1: (2, 3), 2: (4, 5), 3: (6, 7), 4: (8, 12), 5: (13, 14), 8: (9, 10), 9: (11, 15)}


def proj_outputs(l):
    out = [("bias", h, None) for h in range(H_NA)]
    for c in range(10):
        if c in IN_TILES:
            out += [("chan", c, t) for t in enumerate(IN_TILES[c])]
        else:
            out += [("val", c, tt) for tt in range(4)]
    return out


SPLIT = [(kind, l, c) for l in range(DEPTH) for kind, n in (("in", 10), ("gate", 12), ("wo", 4))
         for c in range(n)]
UNITS = KD // KU
UNIT0 = {key: UNITS * n for n, key in enumerate(SPLIT)}


OUTS = [proj_outputs(l) for l in range(DEPTH)]
N_OUT = len(OUTS[0])


def by_act(o):
    return OUTS[0][o][0] != "bias" and o % 2 == 0


N_ACT_OUT = sum(by_act(o) for o in range(N_OUT))
N_DVE_OUT = N_OUT - N_ACT_OUT


def out_count(l, o):
    mine = by_act(o)
    n = sum(by_act(q) == mine for q in range(o + 1))
    return mine, n + l * (N_ACT_OUT if mine else N_DVE_OUT)


def last_out(l, c):
    return l * N_OUT + 1 + max(o for o, x in enumerate(OUTS[l]) if x[0] != "bias" and x[1] == c)


def steps(l):
    out = [("na", h, False) for h in range(H_NA)] + [("win", h, False) for h in range(H_Q)]
    if l < DEPTH - 1:
        out += [("na", h, True) for h in range(H_NA)] + [("win", h, True) for h in range(H_Q)]
    return out


STEPS = [steps(l) for l in range(DEPTH)]
STEP0 = [0, len(STEPS[0])]
QT = [4, 2]
QN = [q * P for q in QT]
QT0 = [0, 4]


def lat_steps(l, s):
    return sum(not x[2] for k in range(l) for x in STEPS[k]) + sum(not x[2] for x in STEPS[l][:s + 1])


def width(l, s):
    family, _, on_ctx = STEPS[l][s]
    return (CTX if on_ctx else NTOK) + (family == "win")


SMALL = 16 * 6


def lin(i, first, per):
    return first if i is None else i * per + first


def program(nc, t, out):
    ctx = ExitStack()
    with ctx:
        def sb(name, shape, dt=F32):
            return ctx.enter_context(nc.sbuf_tensor(name, shape, dt))

        def sem(name):
            return ctx.enter_context(nc.semaphore(name))

        xd = nc.dram_tensor("dispatched", (ROWS_D, D), F32, kind="Internal").ap()
        yd = nc.dram_tensor("expert_rows", (ROWS_D, D), F32, kind="Internal").ap()

        consts = sb("consts", [P, sum(CONST_COLS.values())])
        at, C = 0, {}
        for name, n in CONST_COLS.items():
            C[name] = consts[:, at:at + n]
            at += n
        ident = C["ident"]
        ring = sb("ring", [P, SLOTS, KD * CW])
        X = sb("X", [P, 4, D])
        h_hi = sb("h_hi", [P, KD, NTOK], F32R)
        h_lo = sb("h_lo", [P, KD, NTOK], F32R)
        w_hi = sb("w_hi", [P, AHEAD, KU, CW], F32R)
        w_lo = sb("w_lo", [P, AHEAD, KU, CW], F32R)
        arena = sb("arena", [P, 20, 512])
        modc = sb("modc", [P, 6, D])
        strip = sb("strip", [P, H_NA, 6 * GRID_W])
        att = sb("att", [P, 3 * 2 * 516 + 1024])
        cond = sb("cond", [P, 2, KD])
        cond_s = sb("cond_s", [P, 2, KD])
        cond_bc = sb("cond_bc", [P, KD, P])
        w_router = sb("w_router", [P, KD, NR])
        b_router = sb("b_router", [P, NR])
        sinks_bc = sb("sinks_bc", [P, H_Q])
        convw = sb("convw", [P, 2, CONV_W])
        stat = sb("stat", [P, 24])
        negmax = sb("negmax", [P, 3, 2])
        esum = sb("esum", [P, 3, 2])
        rsum = sb("rsum", [P, 3, 2])
        top_g = sb("top_g", [P, 4, 8])
        idx_g = sb("idx_g", [P, 4, 8], U32)
        top_e = sb("top_e", [P, 4, 8])
        idx_e = sb("idx_e", [P, 4, 8], U32)
        rt = sb("rt", [P, 64])
        slots_f = sb("slots_f", [P, 2, 4])
        slots_u = sb("slots_u", [P, 2, 4], U32)
        wts = sb("wts", [P, 2, 4])
        meta = sb("meta", [1, 1 + SPILL[0]], I32)

        r_hi, r_lo = (w[:, :, :, :].rearrange("p u a b -> p (u a b)")[:, 0:KD * NR].rearrange("p (k n) -> p k n", k=KD)
                      for w in (w_hi, w_lo))

        def tile(n, k=1):
            return arena[:, n:n + k, :].rearrange("p a b -> p (a b)")

        vals = arena[:, 16:20, :]
        htok = arena[:, 12:20, :].rearrange("p (t a) b -> p t (a b)", a=2)
        mT = arena[:, 12:20, :]
        mod_scale = [tile(0, 2), tile(4, 2)]
        mod_shift = [tile(2, 2), tile(6, 2)]
        gate_bc = [tile(2, 2), tile(4, 2)]
        gate_f = [tile(4, 2), tile(6, 2)]
        g_bc = tile(10, 2)
        xe = [arena[0:CAP, 8 + 2 * b:10 + 2 * b, :].rearrange("p a b -> p (a b)") for b in range(2)]
        xe.append(arena[0:CAP, 14:16, :].rearrange("p a b -> p (a b)"))
        xeT = [arena[:, b, :].rearrange("p (k s) -> p k s", k=KD) for b in range(3)]
        act_g = arena[0:CAP, 3, 0:DE]
        hid = arena[0:CAP, 3, DE:2 * DE]
        y_sb = [arena[0:CAP, a:a + 2, :].rearrange("p a b -> p (a b)") for a in (12, 16, 18)]
        hidT = sb("hidT", [P, 2, CAP])
        spill_gu = [att[:, KD * DE * b:KD * DE * (b + 1)] for b in range(2)]
        spill_d = arena[:, 16:20, :].rearrange("p a b -> p (a b)")
        S = [att[:, 1032 * b:1032 * b + 1032].rearrange("p (t c) -> p t c", t=2) for b in range(3)]
        PT = att[:, 3096:4120].rearrange("p (k q) -> p k q", k=4)
        rev = strip[:, :, :].rearrange("p a b -> p (a b)")
        sig = [att[:, 512 * b:512 * b + 512] for b in range(6)]
        got = [[att[:, (2 * b + j) * D:(2 * b + j + 1) * D] for j in range(2)] for b in range(2)]
        got += [[tile(12 + 4 * b + 2 * j, 2) for j in range(2)] for b in range(2)]
        pick = att[:, 0:256].rearrange("p (c t e) -> p c t e", c=2, t=4)
        prod = att[:, 256:512].rearrange("p (c t e) -> p c t e", c=2, t=4)
        both = att[:, 512:640].rearrange("p (t e) -> p t e", t=4)
        rank = att[:, 640:768].rearrange("p (t e) -> p t e", t=4)
        lem = att[:, 768:896].rearrange("p (t e) -> p t e", t=4)
        cnt = att[:, 896:1024]
        lg = att[:, 1024:1024 + 4 * NR].rearrange("p (t e) -> p t e", t=4)
        g8 = att[:, 1280:1312].rearrange("p (t e) -> p t e", t=4)
        lgT = att[0:NR, 3072:3072 + NTOK]
        rope_t = att[:, 2304:2304 + 4 * SEQ].rearrange("p (a b) -> p a b", a=4)
        upd = [att[:, 3072:3328], att[:, 3328:3584], att[:, 3584:3840], att[:, 3840:4096]]

        banks = ctx.enter_context(nc.psum_tensor("banks", [P, 8, 512], F32))

        consts_in = sem("consts_in")
        cond_in = sem("cond_in")
        x_in = sem("x_in")
        small_in = [sem(f"small_in{l}") for l in range(DEPTH)]
        bias_in = [sem(f"bias_in{s}") for s in range(3)]
        g_in = sem("g_in")
        rev_in = sem("rev_in")
        loaded = [sem(f"loaded{s}") for s in range(SLOTS)]
        cond_act = sem("cond_act")
        cond_ready = sem("cond_ready")
        mod_done = sem("mod_done")
        mod_out = sem("mod_out")
        scale_ready = sem("scale_ready")
        shift_ready = sem("shift_ready")
        sq_done = sem("sq_done")
        ms_ready = sem("ms_ready")
        std_ready = sem("std_ready")
        h_scaled = sem("h_scaled")
        h_even = sem("h_even")
        h_odd = sem("h_odd")
        h_turned = sem("h_turned")
        w_hi_ready = sem("w_hi_ready")
        w_lo_ready = sem("w_lo_ready")
        unit_done = sem("unit_done")
        h_hi_ready = sem("h_hi_ready")
        h_lo_ready = sem("h_lo_ready")
        proj_done = sem("proj_done")
        out_act = sem("out_act")
        out_dve = sem("out_dve")
        rope_mm = sem("rope_mm")
        rope_done = sem("rope_done")
        z_ready = sem("z_ready")
        conv_done = sem("conv_done")
        y_a_ready = sem("y_a_ready")
        sc_lat_done = sem("sc_lat_done")
        sc_ctx_done = sem("sc_ctx_done")
        s_dve = sem("s_dve")
        s_act = sem("s_act")
        max_ready = sem("max_ready")
        exp_done = sem("exp_done")
        p_ready = sem("p_ready")
        p_turned = sem("p_turned")
        pt_dve = sem("pt_dve")
        pt_act = sem("pt_act")
        pv_done = sem("pv_done")
        o_ready = sem("o_ready")
        gate_done = sem("gate_done")
        branch_done = sem("branch_done")
        sig_ready = sem("sig_ready")
        gated = sem("gated")
        m_ready = sem("m_ready")
        wo_done = sem("wo_done")
        gate_ready = sem("gate_ready")
        upd_ready = sem("upd_ready")
        x_attn = sem("x_attn")
        x_moe = sem("x_moe")
        m_hi_ready = sem("m_hi_ready")
        m_lo_ready = sem("m_lo_ready")
        router_hi_ready = sem("router_hi_ready")
        router_lo_ready = sem("router_lo_ready")
        lgT_done = sem("lgT_done")
        lgT_out = sem("lgT_out")
        lg_done = sem("lg_done")
        router_exp_in = sem("router_exp_in")
        router_exp = sem("router_exp")
        pick_ready = sem("pick_ready")
        rank_done = sem("rank_done")
        slots_ready = sem("slots_ready")
        meta_ready = sem("meta_ready")
        wts_ready = sem("wts_ready")
        zero_ready = sem("zero_ready")
        xd_zero = sem("xd_zero")
        scattered = sem("scattered")
        xe_in = [sem(f"xe_in{b}") for b in range(3)]
        xe_turned = sem("xe_turned")
        xeT_ready = sem("xeT_ready")
        e_gate_done = sem("e_gate_done")
        e_up_done = sem("e_up_done")
        silu_ready = sem("silu_ready")
        hid_ready = sem("hid_ready")
        hid_turned = sem("hid_turned")
        hidT_ready = sem("hidT_ready")
        down_done = sem("down_done")
        y_out = sem("y_out")
        y_stored = [sem(f"y_stored{b}") for b in range(3)]
        spill_dma = [sem(f"spill_dma{l}") for l in range(DEPTH)]
        spill_out = [sem(f"spill_out{l}") for l in range(DEPTH)]
        spill_step = [sem(f"spill_step{l}") for l in range(DEPTH)]
        rows_done = sem("rows_done")
        got_in = [sem(f"got_in{tt}") for tt in range(4)]
        gate_f_ready = sem("gate_f_ready")
        y_weighted = sem("y_weighted")
        y_gated = sem("y_gated")
        fin_ready = sem("fin_ready")
        stored = sem("stored")
        dve_seq = sem("dve_seq")
        pe_held = sem("pe_held")
        act_seq = sem("act_seq")
        pool_seq = sem("pool_seq")

        def chunk(key):
            return ring[:, AT[key] % SLOTS, :].rearrange("p (k n) -> p k n", n=CW)

        def landed(eng, key, i=None):
            j = AT[key]
            eng.wait_ge(loaded[j % SLOTS], lin(i, LOADED[j], 16 * 3 * UNROLL // SLOTS))

        NORM_TILES = [[0, 1, 2, 3], [0, 1, 2, 3], [0, 1, 2, 3], [0, 1]]
        N0 = [0, 4, 8, 12, 14]

        MOD_BEFORE = [12, 20, 48, 48]

        E0 = [0, NE]
        ZEROED = 16 * (ROWS_D // P + (ROWS_D - MAIN) // P)

        def unit_read(u):
            kind, l, c = SPLIT[u // UNITS]
            if u % UNITS < UNITS - 1:
                return unit_done, (UNITS - 1) * (u // UNITS) + u % UNITS + 1
            if kind == "in":
                return proj_done, last_out(l, c)
            if kind == "gate":
                return gate_done, 24 * l + 2 * c + 2
            return wo_done, 4 * QT0[l] + QT[l] * (c + 1)

        def split_ahead(split, key, following):
            if key:
                for q in range(AHEAD, UNITS):
                    split(key, q)
            if following:
                for q in range(AHEAD):
                    split(following, q)

        def stores(n, b):
            return 16 * ((n - b + 2) // 3)

        def out_place(l, what, c, arg):
            if what == "val":
                return vals[:, arg, (c - 6) * CW:(c - 5) * CW], CW
            n = NTOK if arg[1] >= T_NK else QN[l]
            return arena[:, arg[1], 0:n], n

        block = ctx.enter_context(nc.Block())

        @block.sync
        def _(sp):
            def released(key, i=None):
                kind, l, c = key
                if kind == "mod":
                    return mod_done, 24 * l + c + 1
                if kind in ("in", "gate", "wo"):
                    return w_lo_ready, UNIT0[key] + UNITS
                if kind == "branch":
                    return branch_done, 24 * l + 6 * c + 6
                if kind == "eg":
                    return e_gate_done, lin(i, E0[l] + c + 1, UNROLL)
                if kind == "eu":
                    return e_up_done, lin(i, E0[l] + c + 1, UNROLL)
                return down_done, lin(i, E0[l] + c + 1, UNROLL)

            def load(j, i=None, e=None):
                kind, l, c = STREAM[j]
                dst = chunk(STREAM[j])
                if j >= SLOTS:
                    sp.wait_ge(*released(STREAM[j - SLOTS], i))
                done = loaded[j % SLOTS]
                if kind == "mod":
                    src = t["w_mod"][l].rearrange("(p k) n -> p k n", k=KD)[:, :, c * CW:(c + 1) * CW]
                    sp.dma_start(dst, src).then_inc(done, 16)
                elif kind in ("in", "gate"):
                    src = t["w_in"][l].rearrange("(p k) n -> p k n", k=KD)
                    if kind == "gate":
                        n, b = divmod(c, 3)
                        a = COL_G + b * D + n * CW
                        parts = [(0, a, CW)]
                    elif c <= 5:
                        parts = [(0, c * CW, CW)]
                    elif c == 6:
                        parts = [(0, COL_NV, CW)]
                    elif c == 7:
                        parts = [(0, COL_NV + CW, P), (P, COL_WV, P)]
                    else:
                        heads = [(0, 0), (0, 1), (1, 0), (1, 1)] if c == 8 else [(2, 0), (2, 1)]
                        parts = [(n * HD, COL_WQ + (g * 3 + tt) * HD, HD) for n, (tt, g) in enumerate(heads)]
                        if c == 9:
                            parts.append((P, COL_WK, P))
                    assert len(parts) == pieces(kind, c)
                    for to, fr, n in parts:
                        sp.dma_start(dst[:, :, to:to + n], src[:, :, fr:fr + n]).then_inc(done, 16)
                elif kind == "branch":
                    w = t["w_branch"][l][:, c * CW:(c + 1) * CW]
                    o2 = D_CONV + D_NA
                    sp.dma_start(dst[:, 0:5, :], w[0:o2].rearrange("(k p) n -> p k n", p=P)).then_inc(done, 16)
                    for g in range(2):
                        rows = w[o2 + g * 3 * HD:o2 + (g + 1) * 3 * HD]
                        sp.dma_start(dst[g * HD:(g + 1) * HD, 5:8, :],
                                     rows.rearrange("(t r) n -> r t n", r=HD)).then_inc(done, 16)
                elif kind == "wo":
                    src = t["w_o"][l].rearrange("(k p) n -> p k n", p=P)[:, :, c * CW:(c + 1) * CW]
                    sp.dma_start(dst, src).then_inc(done, 16)
                else:
                    name = {"eg": "w_e_gate", "eu": "w_e_up", "ed": "w_e_down"}[kind]
                    w = t[name][l, c] if e is None else t[name][l][bass.ds(e, 1)].rearrange("a r n -> (a r) n")
                    sp.dma_start(ring[:, j % SLOTS, :], w.rearrange("(p k) n -> p (k n)", p=P)).then_inc(done, 16)

            j = 0
            for l in range(DEPTH):
                first = AT[("eg", l, 4)]
                while j < first:
                    load(j)
                    j += 1
                with sp.Fori(0, LOOPED) as i:
                    for u in range(UNROLL):
                        e1, e0 = sp.snap(i * UNROLL + (4 + u)), sp.snap(i * UNROLL + (3 + u))
                        load(j, i, e1)
                        load(j + 1, i, e1)
                        load(j + 2, i, e0)
                        j += 3
                j = AT[("eg", l, NE - 4)]
                last = AT[("mod", 1, 13) if l == 0 else ("ed", l, NE - 1)]
                while j <= last:
                    load(j)
                    j += 1
                sp.wait_ge(meta_ready, l + 1)
                n_spill = sp.value_load(meta[0:1, 0:1], min_val=0, max_val=SPILL[l])
                with sp.If(n_spill > 0):
                    with sp.Fori(0, SPILL[l]) as b:
                        with sp.If(b < n_spill):
                            e = sp.value_load(meta[0:1, bass.ds(b + 1, 1)], min_val=0, max_val=NE - 1)
                            sp.wait_ge(spill_step[l], b * 9 + 1)
                            for dst, name in ((spill_gu[0], "w_e_gate"), (spill_gu[1], "w_e_up"),
                                              (spill_d, "w_e_down")):
                                w = t[name][l][bass.ds(e, 1)].rearrange("a r n -> (a r) n")
                                sp.dma_start(dst, w.rearrange("(p k) n -> p (k n)", p=P)).then_inc(spill_dma[l], 16)
            while j < len(STREAM):
                load(j)
                j += 1

        @block.gpsimd
        def _(pool):
            seq = [0]

            def link(ins):
                seq[0] += 1
                ins.then_inc(pool_seq, 1)
                pool.wait_ge(pool_seq, seq[0])

            def norm_tail(m):
                pool.wait_ge(shift_ready, m + 1)
                for tt in NORM_TILES[m][0::2]:
                    pool.wait_ge(h_scaled, N0[m] + tt + 1)
                    pool.tensor_tensor(htok[:, tt, :], htok[:, tt, :], mod_shift[tt // 2], ALU.add)\
                        .then_inc(h_even, 1)

            def zero_rows():
                zero = tile(T_AC, 2)
                pool.wait_ge(y_a_ready, 2)
                pool.memset(zero, 0.0).then_inc(zero_ready, 1)
                pool.wait_ge(zero_ready, 1)
                for dst, first in ((xd, 0), (yd, MAIN)):
                    for r in range(first // P, ROWS_D // P):
                        pool.dma_start(dst[r * P:(r + 1) * P, :], zero).then_inc(xd_zero, 16)

            def conv(l):
                n = QN[l]
                for o in (10, 11):
                    mine, count = out_count(l, o)
                    pool.wait_ge(out_act if mine else out_dve, count)
                pool.wait_ge(small_in[l], SMALL)
                for c in range(2):
                    a, g = (arena[:, q + c, 0:n] for q in (T_AH, T_AC))
                    link(pool.tensor_tensor(a, a, g, ALU.mult))
                    pool.tensor_scalar(g, a, convw[:, c, 1:2], None, ALU.mult).then_inc(z_ready, 1)
                for c in range(2):
                    pool.wait_ge(conv_done, 2 * l + c + 1)
                    a, b, g = (arena[:, q + c, 0:n] for q in (T_AH, T_AB, T_AC))
                    pool.tensor_tensor(a, g, b, ALU.mult).then_inc(y_a_ready, 1)

            def merge(l):
                n = QN[l]
                pool.wait_ge(pv_done, STEP0[l] + len(STEPS[l]))
                for q in range(8):
                    pair, half = divmod(q, 2)
                    pool.wait_ge(gated, 24 * l + 6 * pair + 3 * half + 3)
                    s = [sig[2 * b + half][:, 0:n] for b in range(3)]
                    link(pool.tensor_tensor(mT[:, q, 0:n], s[0], s[1], ALU.add))
                    pool.tensor_tensor(mT[:, q, 0:n], mT[:, q, 0:n], s[2], ALU.add).then_inc(m_ready, 1)

            def residual(l):
                for c in range(4):
                    for tt in range(QT[l]):
                        r = c * QT[l] + tt
                        pool.wait_ge(upd_ready, 4 * QT0[l] + r + 1)
                        x = X[:, tt, c * CW:(c + 1) * CW]
                        pool.tensor_tensor(x, x, upd[r % 4], ALU.add).then_inc(x_attn, 1)

            def scatter(l):
                pool.wait_ge(slots_ready, l + 1)
                if l == 0:
                    pool.wait_ge(xd_zero, ZEROED)
                for tt in range(QT[l]):
                    for c in range(2):
                        pool.indirect_dma_start(
                            out=xd, out_offset=bass.IndirectOffsetOnAxis(ap=slots_u[:, c, tt:tt + 1], axis=0),
                            in_=htok[:, tt, :], in_offset=None).then_inc(scattered, 16)

            def combine(l):
                for b in range(3):
                    pool.wait_ge(y_stored[b], stores(E0[l] + NE, b))
                pool.wait_ge(rows_done, l + 1)

                for tt in range(QT[l]):
                    for c in range(2):
                        pool.indirect_dma_start(
                            out=got[tt][c], out_offset=None, in_=yd,
                            in_offset=bass.IndirectOffsetOnAxis(ap=slots_u[:, c, tt:tt + 1], axis=0))\
                            .then_inc(got_in[tt], 16)
                for tt in range(QT[l]):
                    pool.wait_ge(y_gated, QT0[l] + tt + 1)
                    pool.tensor_tensor(X[:, tt, :], X[:, tt, :], got[tt][0], ALU.add).then_inc(x_moe, 1)

            for l in range(DEPTH):
                norm_tail(2 * l)
                conv(l)
                if l == 0:
                    zero_rows()
                merge(l)
                residual(l)
                norm_tail(2 * l + 1)
                scatter(l)
                combine(l)

        @block.tensor
        def _(pe):
            mm, turn = nc.tensor.matmul, nc.tensor.transpose

            def mod(l, c):
                if l == 0 and c == 0:
                    pe.wait_ge(cond_ready, 2)
                landed(pe, ("mod", l, c))
                m = 24 * l + c
                if m >= 4:
                    pe.wait_ge(mod_out, m - 3)
                w = chunk(("mod", l, c))
                for k in range(KD):
                    ins = mm(banks[:, 4 + (c + 2) % 4, 0:CW], cond_bc[:, k, :], w[:, k, :], start=k == 0, stop=k == KD - 1)
                ins.then_inc(mod_done, 1)

            def norm_turn(m):
                if m == 0:
                    pe.wait_ge(consts_in, 16)
                pe.wait_ge(mod_out, MOD_BEFORE[m])
                for n, tt in enumerate(NORM_TILES[m]):
                    pe.wait_ge(h_odd if tt % 2 else h_even, (N0[m] + n) // 2 + 1)
                    for half in range(2):
                        for q in range(4):
                            ins = turn(banks[:, 2 * n + half, q * P:(q + 1) * P], htok[:, tt, 4 * half + q::KD], ident)
                        ins.then_inc(h_turned, 1)
                pe.wait_ge(h_lo_ready, 2 * N0[m + 1])

            def split_units(key, outs, sides, done):
                for q in range(UNITS):
                    u = UNIT0[key] + q
                    pe.wait_ge(w_lo_ready, u + 1)
                    for out_ap, where in outs:
                        for kk in range(KU):
                            k = q * KU + kk
                            for p_, (a, b) in enumerate(sides(u % AHEAD, kk, k, where)):
                                ins = mm(out_ap, a, b, start=k == 0 and p_ == 0, stop=k == KD - 1 and p_ == 2)
                        if q == UNITS - 1:
                            ins.then_inc(done, 1)
                    if q < UNITS - 1:
                        ins.then_inc(unit_done, 1)

            def chan_sides(n):
                def sides(buf, kk, k, half):
                    wh, wl = (w[:, buf, kk, half * P:(half + 1) * P] for w in (w_hi, w_lo))
                    return (wh, h_hi[:, k, 0:n]), (wh, h_lo[:, k, 0:n]), (wl, h_hi[:, k, 0:n])
                return sides

            def val_sides(buf, kk, k, tt):
                hh, hl = (h[:, k, tt * P:(tt + 1) * P] for h in (h_hi, h_lo))
                return (hh, w_hi[:, buf, kk, :]), (hl, w_hi[:, buf, kk, :]), (hh, w_lo[:, buf, kk, :])

            def project(l):
                def bank(o):
                    if o >= 8:
                        mine, count = out_count(l, o - 8)
                        pe.wait_ge(out_act if mine else out_dve, count)
                    return banks[:, o % 8, :]

                pe.wait_ge(rev_in, 16 * 2 * H_NA * (l + 1))
                for h in range(H_NA):
                    mm(bank(h)[:, 0:6 * GRID_W], C["flip"], rev[:, h * 384:(h + 1) * 384], start=True, stop=True)\
                        .then_inc(proj_done, 1)
                for c in range(10):
                    mine = [(o, arg) for o, (what, ch, arg) in enumerate(OUTS[l]) if what != "bias" and ch == c]
                    if c in IN_TILES:
                        n = max(NTOK if tn >= T_NK else QN[l] for _, (_, tn) in mine)
                        split_units(("in", l, c), [(bank(o)[:, 0:n], half) for o, (half, _) in mine],
                                    chan_sides(n), proj_done)
                    else:
                        split_units(("in", l, c), [(bank(o)[:, 0:CW], tt) for o, tt in mine], val_sides, proj_done)
                pe.wait_ge(out_act, (l + 1) * N_ACT_OUT)
                pe.wait_ge(out_dve, (l + 1) * N_DVE_OUT)
                for r, tn in enumerate((T_WQ, T_WQ + 1, T_WQ + 2, T_WK)):
                    mm(banks[:, 4 + r, 0:SEQ], C["rot"], arena[:, tn, 0:SEQ], start=True, stop=True).then_inc(rope_mm, 1)

            def q_place(family, h):
                if family == "na":
                    return T_NQ + h // 2, HD * (h % 2)
                return T_WQ + h % 3, HD * (h // 3)

            def scores(l, s):
                family, h, on_ctx = STEPS[l][s]
                g = STEP0[l] + s
                if s >= 2:
                    pe.wait_ge(s_act, g - 1)
                    pe.wait_ge(s_dve, lat_steps(l, s - 2))
                tn, p0 = q_place(family, h)
                kt = T_NK + h // 2 if family == "na" else T_WK
                q0 = SEQ if on_ctx else 0
                for part in ((1,) if on_ctx else (0, 1)):
                    for b in range(2):
                        ins = mm(banks[:, 2 * (s % 2) + part, b * SEQ:(b + 1) * SEQ],
                                 arena[p0:p0 + HD, tn, q0 + b * P:q0 + (b + 1) * P],
                                 arena[p0:p0 + HD, kt, part * SEQ:(part + 1) * SEQ], start=True, stop=True)
                    ins.then_inc(sc_ctx_done if part else sc_lat_done, 1)

            def turn_p(l, s):
                on_ctx = STEPS[l][s][2]
                g = STEP0[l] + s
                pe.wait_ge(p_ready, g + 1)
                if g:
                    pe.wait_ge(pt_dve, g)
                    pe.wait_ge(pt_act, g)
                for b in range(2):
                    for q in range(2 if on_ctx else 4):
                        ins = turn(banks[:, 4 + b, q * P:(q + 1) * P], S[s % 3][:, b, q * P:(q + 1) * P], ident)
                ins.then_inc(p_turned, 1)

            def attend(l, s):
                family, h, on_ctx = STEPS[l][s]
                g = STEP0[l] + s
                pe.wait_ge(pt_dve, g + 1)
                pe.wait_ge(pt_act, g + 1)
                if g >= 2:
                    pe.wait_ge(o_ready, g - 1)
                v0 = h * HD if family == "na" else D_NA + (h // 3) * HD
                t0, n = (2, 2) if on_ctx else (0, 4)
                for q in range(n):
                    ins = mm(banks[0:HD, 6 + s % 2, 0:2 * P], vals[:, t0 + q, v0:v0 + HD], PT[:, q, :],
                             start=q == 0, stop=q == n - 1)
                ins.then_inc(pv_done, 1)

            def attention(l):
                n = len(STEPS[l])
                for s in range(-1, n + 2):
                    if s == 1:
                        pe.wait_ge(rope_done, 4 * (l + 1))
                    if s + 1 < n:
                        scores(l, s + 1)
                    if 0 <= s - 2 < n:
                        attend(l, s - 2)
                    if 0 <= s - 1 < n:
                        turn_p(l, s - 1)

            BRANCH = [(0, 1), (2, 3, 4), (5, 6, 7)]
            Y_TILE = [T_AH, T_AH + 1, T_NQ, T_NQ + 1, T_NQ + 2, T_WQ, T_WQ + 1, T_WQ + 2]

            def merge(l):
                n = QN[l]
                pe.wait_ge(o_ready, STEP0[l] + len(STEPS[l]))
                pe.wait_ge(y_a_ready, 2 * (l + 1))

                def bank(pair, r):
                    q = 12 * pair + r
                    if q >= 8:
                        pr, rr = divmod(q - 8, 12)
                        if rr < 6:
                            pe.wait_ge(sig_ready, 24 * l + 6 * pr + rr + 1)
                        else:
                            pe.wait_ge(gated, 24 * l + 6 * pr + rr - 6 + 1)
                    return banks[:, q % 8, 0:n]

                for pair in range(4):
                    for b in range(3):
                        split_units(("gate", l, 3 * pair + b), [(bank(pair, 2 * b + half), half) for half in range(2)],
                                    chan_sides(n), gate_done)
                    landed(pe, ("branch", l, pair))
                    w = chunk(("branch", l, pair))
                    for half in range(2):
                        for b in range(3):
                            o = bank(pair, 6 + 3 * half + b)
                            for k in BRANCH[b]:
                                ins = mm(o, w[:, k, half * P:(half + 1) * P], arena[:, Y_TILE[k], 0:n],
                                         start=k == BRANCH[b][0], stop=k == BRANCH[b][-1])
                            ins.then_inc(branch_done, 1)

            def out_proj(l):
                pe.wait_ge(m_lo_ready, 8 * (l + 1))
                for c in range(4):
                    outs = []
                    for tt in range(QT[l]):
                        r = c * QT[l] + tt
                        if r >= 8:
                            pe.wait_ge(upd_ready, 4 * QT0[l] + r - 7)
                        outs.append((banks[:, r % 8, 0:CW], tt))
                    split_units(("wo", l, c), outs, val_sides, wo_done)

            def route(l):
                pe.wait_ge(router_lo_ready, l + 1)
                n = QN[l]
                for k in range(KD):
                    for p_, (a, b) in enumerate(((r_hi, h_hi), (r_hi, h_lo), (r_lo, h_hi))):
                        ins = mm(banks[0:NR, 2, 0:n], a[:, k, :], b[:, k, 0:n],
                                 start=k == 0 and p_ == 0, stop=k == KD - 1 and p_ == 2)
                ins.then_inc(lgT_done, 1)
                pe.wait_ge(lgT_out, l + 1)
                hold()
                for tt in range(QT[l]):
                    ins = turn(banks[:, 0, tt * NR:(tt + 1) * NR], lgT[:, tt * P:(tt + 1) * P], ident[0:NR, 0:NR])
                ins.then_inc(lg_done, 1)

            def ranks(l):
                pe.wait_ge(pick_ready, l + 1)
                for tt in range(QT[l]):
                    for u in range(tt + 1):
                        mm(banks[:, 1, tt * NE:(tt + 1) * NE], C["upper"] if u == tt else C["ones"], both[:, u, :],
                           start=u == 0, stop=u == tt)
                for u in range(QT[l]):
                    ins = mm(banks[:, 1, 4 * NE:5 * NE], C["ones"], both[:, u, :], start=u == 0, stop=u == QT[l] - 1)
                ins.then_inc(rank_done, 1)

            def hold():
                pe.nop().then_inc(pe_held, 1)

            def turn_x(b):
                for k in range(KD):
                    ins = turn(banks[:, 0, k * CAP:(k + 1) * CAP], xe[b][:, k::KD], ident[0:CAP, 0:CAP])
                return ins

            def gate_up(b, w, o):
                for k in range(KD):
                    ins = mm(banks[0:CAP, o, 0:DE], xeT[b][:, k, :], w[:, k * DE:(k + 1) * DE],
                             start=k == 0, stop=k == KD - 1)
                return ins

            def turn_hid():
                for k in range(2):
                    ins = turn(banks[:, 1, k * CAP:(k + 1) * CAP], hid[:, k::2], ident[0:CAP, 0:CAP])
                return ins

            def down(w):
                for half in range(2):
                    for k in range(2):
                        ins = mm(banks[0:CAP, 4 + half, :], hidT[:, k, :], w[:, k * D + half * 512:k * D + half * 512 + 512],
                                 start=k == 0, stop=k == 1)
                return ins

            def slot_of(key):
                return ring[:, AT[key] % SLOTS, :]

            def step_x(l, e, i=None):
                n = E0[l] + e
                pe.wait_ge(xe_in[n % 3], lin(i, 16 * (n // 3 + 1), 16 * UNROLL // 3))
                if n:
                    pe.wait_ge(xeT_ready, lin(i, n, UNROLL))
                hold()
                turn_x(n % 3).then_inc(xe_turned, 1)

            def step_gu(l, e, i=None):
                n = E0[l] + e
                landed(pe, ("eg", l, e), i)
                if n:
                    pe.wait_ge(hid_ready, lin(i, n, UNROLL))
                pe.wait_ge(xeT_ready, lin(i, n + 1, UNROLL))
                gate_up(n % 3, slot_of(("eg", l, e)), 2).then_inc(e_gate_done, 1)
                landed(pe, ("eu", l, e), i)
                gate_up(n % 3, slot_of(("eu", l, e)), 3).then_inc(e_up_done, 1)

            def step_h(l, e, i=None):
                n = E0[l] + e
                if n:
                    pe.wait_ge(hidT_ready, lin(i, n, UNROLL))
                pe.wait_ge(hid_ready, lin(i, n + 1, UNROLL))
                hold()
                turn_hid().then_inc(hid_turned, 1)

            def step_d(l, e, i=None):
                n = E0[l] + e
                landed(pe, ("ed", l, e), i)
                if n:
                    pe.wait_ge(y_out, lin(i, n, UNROLL))
                pe.wait_ge(hidT_ready, lin(i, n + 1, UNROLL))
                down(slot_of(("ed", l, e))).then_inc(down_done, 1)

            def expert_step(l, e, i=None):
                step_h(l, e, i)
                if e + 2 < NE:
                    step_x(l, e + 2, i)
                if e + 1 < NE:
                    step_gu(l, e + 1, i)
                step_d(l, e, i)

            def experts(l):
                pe.wait_ge(mod_out, 36 if l == 0 else 48)
                step_x(l, 0)
                step_x(l, 1)
                step_gu(l, 0)
                for e in range(3):
                    expert_step(l, e)
                with pe.Fori(0, LOOPED) as i:
                    for e in range(3, 3 + UNROLL):
                        expert_step(l, e, i)
                for e in range(NE - 5, NE):
                    expert_step(l, e)

            def spill(l):
                pe.wait_ge(meta_ready, l + 1)
                pe.wait_ge(y_out, E0[l] + NE)
                n_spill = pe.value_load(meta[0:1, 0:1], min_val=0, max_val=SPILL[l])
                with pe.If(n_spill > 0):
                    with pe.Fori(0, SPILL[l]) as b:
                        with pe.If(b < n_spill):
                            step = spill_step[l]
                            pe.wait_ge(spill_dma[l], b * 64 + 64)
                            hold()
                            turn_x(0).then_inc(step, 1)
                            pe.wait_ge(step, b * 9 + 3)
                            gate_up(0, spill_gu[0], 2)
                            gate_up(0, spill_gu[1], 3).then_inc(step, 1)
                            pe.wait_ge(step, b * 9 + 6)
                            hold()
                            turn_hid().then_inc(step, 1)
                            pe.wait_ge(step, b * 9 + 8)
                            down(spill_d).then_inc(step, 1)
                    pe.wait_ge(step, n_spill * 9 + 1)
                    hold()

            for l in range(DEPTH):
                if l == 0:
                    for c in range(12):
                        mod(0, c)
                norm_turn(2 * l)
                project(l)
                attention(l)
                merge(l)
                out_proj(l)
                pe.wait_ge(upd_ready, 4 * (QT0[l] + QT[l]))
                if l == 0:
                    for c in range(12, 20):
                        mod(0, c)
                norm_turn(2 * l + 1)
                route(l)
                if l == 0:
                    for c in range(20, 24):
                        mod(0, c)
                ranks(l)
                if l == 0:
                    for c in range(12):
                        mod(1, c)
                experts(l)
                if l == 0:
                    for c in (12, 13):
                        mod(1, c)
                spill(l)
                if l == 0:
                    for c in range(14, 24):
                        mod(1, c)

        @block.scalar
        def _(act):
            seq = [0]
            fn = nc.scalar.activation

            def link(ins):
                seq[0] += 1
                ins.then_inc(act_seq, 1)
                act.wait_ge(act_seq, seq[0])

            def small_loads(l):
                for dst, src in (
                    (sinks_bc[:, :], t["sinks"][l].partition_broadcast(P)),
                    (convw[:, :, :], t["conv_w"][l].rearrange("(c p) j -> p c j", p=P)),
                    (w_router[:, :, 0:NG], t["w_rg"][l].rearrange("(p k) n -> p k n", k=KD)),
                    (w_router[:, :, NG:NR], t["w_re"][l].rearrange("(p k) n -> p k n", k=KD)),
                    (b_router[:, 0:NG], t["b_rg"][l].partition_broadcast(P)),
                    (b_router[:, NG:NR], t["b_re"][l].partition_broadcast(P)),
                ):
                    act.dma_start(dst, src).then_inc(small_in[l], 16)

            def load_g(m):
                src = [t["g_attn"][0], t["g_ffn"][0], t["g_attn"][1], t["g_ffn"][1], t["g_final"]][m]
                act.dma_start(g_bc, src.partition_broadcast(P)).then_inc(g_in, 16)

            def load_rev(l, heads=range(H_NA)):
                for r in range(2):
                    for h in heads:
                        off = ((l * H_NA + h) * RPB_R + 5 - r) * RPB_C - 48
                        src = bass.AP(t["rpb"].tensor, off, [[1, GRID_W], [RPB_C, 6], [1, GRID_W]])
                        dst = rev[r * GRID_W:(r + 1) * GRID_W, h * 384:(h + 1) * 384]
                        act.dma_start(dst.rearrange("p (j c) -> p j c", j=6), src).then_inc(rev_in, 16)

            act.dma_start(cond[:, 0, :], t["c"][0].rearrange("(p k) -> p k", k=KD)).then_inc(cond_in, 16)
            act.dma_start(cond[:, 1, :], t["c_ctx"].rearrange("(p k) -> p k", k=KD)).then_inc(cond_in, 16)
            def load_bias(l, sec):
                act.dma_start(modc[:, sec, :], t["b_mod"][l][sec * D:(sec + 1) * D].partition_broadcast(P))\
                   .then_inc(bias_in[sec % 3], 16)

            load_bias(0, 0)
            act.wait_ge(cond_in, 32)
            fn(cond_s[:, :, :], cond[:, :, :], ACT.Silu).then_inc(cond_act, 1)
            act.wait_ge(mod_done, 1)
            load_bias(0, 1)
            act.wait_ge(mod_done, 2)
            act.dma_start(X[:, 0:2, :], t["x"][0].rearrange("(t p) d -> p t d", p=P)).then_inc(x_in, 16)
            act.wait_ge(mod_done, 4)
            act.dma_start(X[:, 2:4, :], t["ctx"][0].rearrange("(t p) d -> p t d", p=P)).then_inc(x_in, 16)
            load_g(0)
            act.wait_ge(mod_done, 6)
            load_bias(0, 2)
            act.dma_start(consts[:, :], t["consts"]).then_inc(consts_in, 16)
            small_loads(0)
            load_rev(0)

            def spread(dst, section, s):
                for half in range(2):
                    ins = fn(dst[64 * half:64 * half + 64, :], modc[64 * s:64 * s + 64, section, :], ACT.Copy)
                return ins

            def root_table():
                fn(stat[:, 16:17], ident[:, 0:1], ACT.Sqrt)

            def streams(m):
                return 1 if m == 3 else 2

            def norm(m):
                l, ffn = divmod(m, 2)
                if m >= 1:
                    act.wait_ge(scale_ready, m)
                    if ffn:
                        act.wait_ge(branch_done, 24 * (l + 1))
                        load_g(m)
                    root_table()
                for n, tt in enumerate(NORM_TILES[m]):
                    if m == 0:
                        act.wait_ge(x_in, 32)
                    elif ffn:
                        act.wait_ge(x_attn, 4 * QT0[l] + 3 * QT[l] + tt + 1)
                        if n == 0:
                            act.wait_ge(wo_done, 4 * (QT0[l] + QT[l]))
                    else:
                        act.wait_ge(x_moe, tt + 1)
                    ins = fn(got[tt][0] if m == 2 else htok[:, tt, :], X[:, tt, :], ACT.Square,
                             accum_out=stat[:, tt:tt + 1])
                    ins.then_inc(sq_done, 1)
                act.wait_ge(ms_ready, m + 1)
                fn(stat[:, 8:12], stat[:, 4:8], ACT.Sqrt).then_inc(std_ready, 1)
                act.wait_ge(mod_out, 12 * m + 4)
                if ffn:
                    act.wait_ge(upd_ready, 4 * (QT0[l] + QT[l]))
                for s in range(streams(m)):
                    ins = spread(mod_shift[s], 3 * ffn, s)
                ins.then_inc(shift_ready, 1)
                if ffn:
                    act.wait_ge(small_in[l], SMALL)
                    act.wait_ge(*unit_read(UNIT0[("wo", l, 3)] + UNITS - 1))
                    fn(r_hi, w_router[:, :, :], ACT.Copy).then_inc(router_hi_ready, 1)
                for n, tt in enumerate(NORM_TILES[m]):
                    for half in range(2):
                        act.wait_ge(h_turned, 2 * (N0[m] + n) + half + 1)
                        fn(h_hi[:, 4 * half:4 * half + 4, tt * P:(tt + 1) * P],
                           banks[:, 2 * n + half, :].rearrange("p (k s) -> p k s", k=4), ACT.Copy).then_inc(h_hi_ready, 1)

            def split_w(key, q):
                u = UNIT0[key] + q
                if q == 0:
                    landed(act, key)
                if u >= AHEAD:
                    act.wait_ge(*unit_read(u - AHEAD))
                fn(w_hi[:, u % AHEAD, :, :], chunk(key)[:, q * KU:(q + 1) * KU, :], ACT.Copy).then_inc(w_hi_ready, 1)

            def project(l):
                split_ahead(split_w, None, ("in", l, 0))
                for ch in range(10):
                    split_ahead(split_w, ("in", l, ch), ("in", l, ch + 1) if ch < 9 else ("gate", l, 0))
                    for o, (what, c, arg) in enumerate(OUTS[l]):
                        if by_act(o) and c == ch:
                            act.wait_ge(proj_done, l * N_OUT + o + 1)
                            dst, n = out_place(l, what, c, arg)
                            fn(dst, banks[:, o % 8, 0:n], ACT.Copy).then_inc(out_act, 1)

            def attention(l):
                n = len(STEPS[l])
                for s in range(n + 3):
                    g = STEP0[l] + s
                    if 0 <= s - 1 < n:
                        b = (s - 1) % 3
                        act.wait_ge(max_ready, g)
                        w = width(l, s - 1)
                        for q in range(2):
                            ins = fn(S[b][:, q, 0:w], S[b][:, q, 0:w], ACT.Exp, bias=negmax[:, b, q:q + 1],
                                     accum_out=esum[:, b, q:q + 1])
                        ins.then_inc(exp_done, 1)
                    if 0 <= s - 2 < n:
                        k = 2 if STEPS[l][s - 2][2] else 4
                        act.wait_ge(p_turned, g - 1)
                        if g - 2 > 0:
                            act.wait_ge(pv_done, g - 2)
                        fn(PT[:, 0:k, P:2 * P], banks[:, 5, 0:k * P].rearrange("p (k q) -> p k q", k=k), ACT.Copy)\
                            .then_inc(pt_act, 1)
                    if s < n:
                        on_ctx = STEPS[l][s][2]
                        act.wait_ge(sc_ctx_done, g + 1)
                        if g >= 3:
                            act.wait_ge(p_turned, g - 2)
                        k0 = 0 if on_ctx else SEQ
                        fn(S[s % 3][:, :, k0:k0 + CTX], banks[:, 2 * (s % 2) + 1, :].rearrange("p (b k) -> p b k", b=2), ACT.Copy,
                           scale=SCALE).then_inc(s_act, 1)
                    if 0 <= s - 3 < n:
                        family, h, on_ctx = STEPS[l][s - 3]
                        tn, p0 = (T_NQ + h // 2, HD * (h % 2)) if family == "na" else (T_WQ + h % 3, HD * (h // 3))
                        q0 = SEQ if on_ctx else 0
                        act.wait_ge(pv_done, g - 2)
                        fn(arena[p0:p0 + HD, tn, q0:q0 + 2 * P], banks[0:HD, 6 + (s - 3) % 2, 0:2 * P], ACT.Copy)\
                            .then_inc(o_ready, 1)

            def gates(l):
                n = QN[l]
                for pair in range(4):
                    for r in range(6):
                        g = 3 * pair + r // 2
                        if r % 2 == 0:
                            split_ahead(split_w, ("gate", l, g), ("gate", l, g + 1) if g < 11 else ("wo", l, 0))
                        act.wait_ge(gate_done, 24 * l + 6 * pair + r + 1)
                        if pair:
                            act.wait_ge(m_ready, 8 * l + 2 * (pair - 1) + r % 2 + 1)
                        fn(sig[r][:, 0:n], banks[:, (12 * pair + r) % 8, 0:n], ACT.Sigmoid).then_inc(sig_ready, 1)
                    if pair == 1:
                        act.wait_ge(y_a_ready, 2 * (l + 1))
                        act.wait_ge(xd_zero, ZEROED)
                        for s in range(2 - l):
                            ins = spread(gate_bc[s], 2, s)
                        ins.then_inc(gate_ready, 1)
                for q in range(8):
                    act.wait_ge(m_ready, 8 * l + q + 1)
                    fn(h_hi[:, q, 0:n], mT[:, q, 0:n], ACT.Copy).then_inc(m_hi_ready, 1)
                if l == 0:
                    for sec in range(3, 6):
                        load_bias(0, sec)

            def out_proj(l):
                for c in range(4):
                    split_ahead(split_w, ("wo", l, c), ("wo", l, c + 1) if c < 3 else None)

            def route(l):
                nt = QT[l]
                act.wait_ge(lgT_done, l + 1)
                fn(lgT[:, 0:QN[l]], banks[0:NR, 2, 0:QN[l]], ACT.Copy).then_inc(lgT_out, 1)
                if l == 0:
                    act.wait_ge(gate_ready, 1)
                    for sec in range(3):
                        load_bias(1, sec)
                for r, (dst, src) in enumerate((
                    (prod[:, 0, 0:nt, 0:8], prod[:, 0, 0:nt, 0:8]),
                    (rt[:, 16:16 + nt], rt[:, 12:12 + nt]),
                )):
                    act.wait_ge(router_exp_in, 2 * l + r + 1)
                    fn(dst, src, ACT.Exp).then_inc(router_exp, 1)

            def silu(l, e, i=None):
                n = E0[l] + e
                if n:
                    act.wait_ge(hid_ready, lin(i, n, UNROLL))
                act.wait_ge(e_gate_done, lin(i, n + 1, UNROLL))
                fn(act_g, banks[0:CAP, 2, 0:DE], ACT.Silu).then_inc(silu_ready, 1)

            def store_y(l, e, i=None):
                n = E0[l] + e
                row = e * CAP if i is None else act.snap(i * (UNROLL * CAP) + e * CAP)
                row2 = (e + 5) * CAP if i is None else act.snap(i * (UNROLL * CAP) + (e + 5) * CAP)
                b = n % 3
                if n >= 3:
                    act.wait_ge(y_stored[b], lin(i, stores(n, b), 16 * UNROLL // 3))
                act.wait_ge(down_done, lin(i, n + 1, UNROLL))
                fn(y_sb[b], banks[0:CAP, 4:6, :].rearrange("p a b -> p (a b)"), ACT.Copy).then_inc(y_out, 1)
                act.wait_ge(y_out, lin(i, n + 1, UNROLL))
                act.dma_start(yd[bass.ds(row, CAP), :], y_sb[b]).then_inc(y_stored[b], 16)
                if e + 5 < NE:
                    act.wait_ge(xe_turned, lin(i, n + 3, UNROLL))
                    act.dma_start(xe[(n + 5) % 3], xd[bass.ds(row2, CAP), :]).then_inc(xe_in[(n + 5) % 3], 16)

            def experts(l):
                act.wait_ge(xd_zero, ZEROED)
                act.wait_ge(scattered, 32 * (QT0[l] + QT[l]))
                for e in range(5 - 2):
                    n = E0[l] + e
                    act.dma_start(xe[n % 3], xd[e * CAP:(e + 1) * CAP, :]).then_inc(xe_in[n % 3], 16)
                act.wait_ge(mod_out, 24 * (l + 1))
                for s in range(2 - l):
                    ins = spread(gate_f[s], 5, s)
                ins.then_inc(gate_f_ready, 1)
                if l == 0:
                    small_loads(1)
                for e in (3, 4):
                    n = E0[l] + e
                    act.wait_ge(xe_turned, n - 2)
                    act.dma_start(xe[n % 3], xd[e * CAP:(e + 1) * CAP, :]).then_inc(xe_in[n % 3], 16)
                silu(l, 0)
                for e in range(3):
                    silu(l, e + 1)
                    store_y(l, e)
                with act.Fori(0, LOOPED) as i:
                    for e in range(3, 3 + UNROLL):
                        silu(l, e + 1, i)
                        store_y(l, e, i)
                for e in range(NE - 5, NE):
                    if e + 1 < NE:
                        silu(l, e + 1)
                    if e == NE - 1:
                        act.wait_ge(scale_ready, 2 * (l + 1))
                        act.wait_ge(xe_turned, E0[l] + NE)
                        load_g(2 * (l + 1))
                    store_y(l, e)
                    if l == 0 and e < 30:
                        if e == 27:
                            act.wait_ge(gate_f_ready, 1)
                            act.wait_ge(mod_out, 36)
                            act.wait_ge(s_dve, lat_steps(0, len(STEPS[0]) - 1))
                        load_bias(1, e - 24)
                        load_rev(1, range(2 * (e - 27), 2 * (e - 27) + 2))

            def spill(l):
                act.wait_ge(meta_ready, l + 1)
                for b in range(3):
                    act.wait_ge(y_stored[b], stores(E0[l] + NE, b))
                n_spill = act.value_load(meta[0:1, 0:1], min_val=0, max_val=SPILL[l])
                step = spill_step[l]
                with act.If(n_spill > 0):
                    act.wait_ge(xe_turned, E0[l] + NE)
                    act.nop().then_inc(step, 1)
                    act.nop().then_inc(spill_out[l], 16)
                    with act.Fori(0, SPILL[l]) as b:
                        with act.If(b < n_spill):
                            row = act.snap(b * CAP + MAIN)
                            act.wait_ge(step, b * 9 + 1)
                            act.dma_start(xe[0], xd[bass.ds(row, CAP), :]).then_inc(spill_dma[l], 16)
                            act.wait_ge(step, b * 9 + 4)
                            fn(act_g, banks[0:CAP, 2, 0:DE], ACT.Silu).then_inc(step, 1)
                            act.wait_ge(spill_out[l], b * 16 + 16)
                            act.wait_ge(step, b * 9 + 9)
                            fn(y_sb[0], banks[0:CAP, 4:6, :].rearrange("p a b -> p (a b)"), ACT.Copy).then_inc(step, 1)
                            act.wait_ge(step, b * 9 + 10)
                            act.dma_start(yd[bass.ds(row, CAP), :], y_sb[0]).then_inc(spill_out[l], 16)
                    act.wait_ge(spill_out[l], n_spill * 16 + 16)
                    act.nop().then_inc(step, 1)
                act.nop().then_inc(rows_done, 1)

            def weigh(l, tt):
                act.wait_ge(got_in[tt], 32 * (l + 1))
                if tt == 0:
                    act.wait_ge(wts_ready, l + 1)
                fn(got[tt][1], got[tt][1], ACT.Copy, scale=wts[:, 1, tt:tt + 1]).then_inc(y_weighted, 1)

            for l in range(DEPTH):
                norm(2 * l)
                project(l)
                attention(l)
                gates(l)
                out_proj(l)
                norm(2 * l + 1)
                route(l)
                experts(l)
                spill(l)
                for tt in range(QT[l]):
                    weigh(l, tt)

            root_table()
            for tt in range(2):
                act.wait_ge(x_moe, QT0[1] + tt + 1)
                fn(htok[:, tt, :], X[:, tt, :], ACT.Square, accum_out=stat[:, tt:tt + 1]).then_inc(sq_done, 1)
            act.wait_ge(ms_ready, 5)
            fn(stat[:, 8:12], stat[:, 4:8], ACT.Sqrt).then_inc(std_ready, 1)
            for tt in range(2):
                act.wait_ge(fin_ready, tt + 1)
                act.dma_start(out[0, tt * P:(tt + 1) * P, :], htok[:, tt, :]).then_inc(stored, 16)
            act.wait_ge(stored, 32)

        @block.vector
        def _(dve):
            v = nc.vector
            seq = [0]

            def link(ins):
                seq[0] += 1
                ins.then_inc(dve_seq, 1)
                dve.wait_ge(dve_seq, seq[0])

            dve.wait_ge(cond_act, 1)
            for s in range(2):
                v.tensor_copy(cond_bc[:, :, 64 * s:64 * s + 64],
                              cond_s[:, s, :].unsqueeze(2).to_broadcast([P, KD, 64])).then_inc(cond_ready, 1)

            def mod_add(l, c):
                m = 24 * l + c
                sec, q = divmod(c, 4)
                if q == 0:
                    dve.wait_ge(bias_in[sec % 3], 16 * (2 * l + c // 12 + 1))
                dve.wait_ge(mod_done, m + 1)
                dst = modc[:, sec, q * CW:(q + 1) * CW]
                v.tensor_tensor(dst, banks[:, 4 + (c + 2) % 4, 0:CW], dst, ALU.add).then_inc(mod_out, 1)

            def rstd(m, tiles):
                dve.wait_ge(sq_done, N0[m] + len(tiles))
                v.tensor_scalar(stat[:, 4:8], stat[:, 0:4], 1.0 / D, EPS, ALU.mult, ALU.add).then_inc(ms_ready, 1)
                dve.wait_ge(std_ready, m + 1)
                link(v.reciprocal(stat[:, 12:16], stat[:, 8:12]))

            def scales(m):
                l, ffn = divmod(m, 2)
                sec = 3 * ffn + 1
                dve.wait_ge(g_in, 16 * (m + 1))
                dve.wait_ge(mod_out, 12 * m + 8)
                ins = v.scalar_tensor_tensor(modc[:, sec, :], modc[:, sec, :], 1.0, g_bc, ALU.add, ALU.mult)
                ins.then_inc(scale_ready, 1)
                dve.wait_ge(scale_ready, m + 1)
                if ffn:
                    dve.wait_ge(xd_zero, ZEROED)
                    dve.wait_ge(branch_done, 24 * (l + 1))
                    dve.wait_ge(upd_ready, 4 * (QT0[l] + QT[l]))
                for s in range(1 if m == 3 else 2):
                    for half in range(2):
                        link(v.tensor_copy(mod_scale[s][64 * half:64 * half + 64, :], modc[64 * s:64 * s + 64, sec, :]))

            def norm(m):
                l, ffn = divmod(m, 2)
                if ffn:
                    dve.wait_ge(router_hi_ready, l + 1)
                    v.tensor_tensor(r_lo, w_router[:, :, :], r_hi.bitcast(F32), ALU.subtract)\
                        .then_inc(router_lo_ready, 1)
                for n, tt in enumerate(NORM_TILES[m]):
                    v.scalar_tensor_tensor(htok[:, tt, :], X[:, tt, :], stat[:, 12 + tt:13 + tt], mod_scale[tt // 2],
                                           ALU.mult, ALU.mult).then_inc(h_scaled, 1)
                    if tt % 2:
                        dve.wait_ge(shift_ready, m + 1)
                        dve.wait_ge(h_scaled, N0[m] + n + 1)
                        v.tensor_tensor(htok[:, tt, :], htok[:, tt, :], mod_shift[tt // 2], ALU.add)\
                            .then_inc(h_odd, 1)
                for n, tt in enumerate(NORM_TILES[m]):
                    for half in range(2):
                        dve.wait_ge(h_hi_ready, 2 * (N0[m] + n) + half + 1)
                        place = slice(4 * half, 4 * half + 4), slice(tt * P, (tt + 1) * P)
                        v.tensor_tensor(h_lo[:, place[0], place[1]],
                                        banks[:, 2 * n + half, :].rearrange("p (k s) -> p k s", k=4),
                                        h_hi[:, place[0], place[1]].bitcast(F32), ALU.subtract).then_inc(h_lo_ready, 1)

            def split_w(key, q):
                u = UNIT0[key] + q
                dve.wait_ge(w_hi_ready, u + 1)
                v.tensor_tensor(w_lo[:, u % AHEAD, :, :], chunk(key)[:, q * KU:(q + 1) * KU, :],
                                w_hi[:, u % AHEAD, :, :].bitcast(F32), ALU.subtract).then_inc(w_lo_ready, 1)

            def project(l):
                split_ahead(split_w, None, ("in", l, 0))
                for h in range(H_NA):
                    dve.wait_ge(proj_done, l * N_OUT + h + 1)
                    v.tensor_tensor(strip[:, h, :].rearrange("p (j c) -> p j c", j=6),
                                    banks[:, h, 0:384].rearrange("p (j c) -> p j c", j=6),
                                    C["mask_na"].unsqueeze(1).to_broadcast([P, 6, GRID_W]), ALU.add)\
                        .then_inc(out_dve, 1)
                for ch in range(10):
                    split_ahead(split_w, ("in", l, ch), ("in", l, ch + 1) if ch < 9 else ("gate", l, 0))
                    for o, (what, c, arg) in enumerate(OUTS[l]):
                        if what != "bias" and c == ch and not by_act(o):
                            dve.wait_ge(proj_done, l * N_OUT + o + 1)
                            dst, n = out_place(l, what, c, arg)
                            v.tensor_copy(dst, banks[:, o % 8, 0:n]).then_inc(out_dve, 1)
                ns = 2 - l
                for c in range(2):
                    dve.wait_ge(z_ready, 2 * l + c + 1)
                    z, a = (arena[:, q + c, 0:256 * ns].rearrange("p (s n) -> p s n", s=ns) for q in (T_AH, T_AC))
                    link(v.scalar_tensor_tensor(a[:, :, 1:256], z[:, :, 0:255], convw[:, c, 0:1], a[:, :, 1:256],
                                                ALU.mult, ALU.add))
                    v.scalar_tensor_tensor(a[:, :, 0:255], z[:, :, 1:256], convw[:, c, 2:3], a[:, :, 0:255],
                                           ALU.mult, ALU.add).then_inc(conv_done, 1)
                for r, tn in enumerate((T_WQ, T_WQ + 1, T_WQ + 2, T_WK)):
                    x = arena[:, tn, 0:SEQ]
                    dve.wait_ge(rope_mm, 4 * l + r + 1)
                    link(v.tensor_tensor(rope_t[:, r, :], x, C["cos"], ALU.mult))
                    link(v.tensor_tensor(x, banks[:, 4 + r, 0:SEQ], C["sin"], ALU.mult))
                    v.tensor_tensor(x, x, rope_t[:, r, :], ALU.add).then_inc(rope_done, 1)

            def attention(l):
                n = len(STEPS[l])
                for s in range(n + 2):
                    g = STEP0[l] + s
                    if 0 <= s - 2 < n:
                        k = 2 if STEPS[l][s - 2][2] else 4
                        dve.wait_ge(p_turned, g - 1)
                        if g - 2 > 0:
                            dve.wait_ge(pv_done, g - 2)
                        v.tensor_copy(PT[:, 0:k, 0:P], banks[:, 4, 0:k * P].rearrange("p (k q) -> p k q", k=k))\
                            .then_inc(pt_dve, 1)
                    if s < n:
                        family, h, on_ctx = STEPS[l][s]
                        buf = S[s % 3]
                        w = width(l, s)
                        if g >= 3:
                            dve.wait_ge(p_turned, g - 2)
                        if not on_ctx:
                            dve.wait_ge(sc_lat_done, lat_steps(l, s))
                            for b in range(2):
                                if family == "na":
                                    add = strip[:, h, (2 - 2 * b) * GRID_W:(6 - 2 * b) * GRID_W]
                                else:
                                    add = C["mask_win"][:, b * SEQ:(b + 1) * SEQ]
                                ins = v.scalar_tensor_tensor(buf[:, b, 0:SEQ], banks[:, 2 * (s % 2), b * SEQ:(b + 1) * SEQ],
                                                             SCALE, add, ALU.mult, ALU.add)
                            ins.then_inc(s_dve, 1)
                        if family == "win":
                            link(v.tensor_copy(buf[:, :, w - 1:w],
                                               sinks_bc[:, h:h + 1].unsqueeze(1).to_broadcast([P, 2, 1])))
                    if 0 <= s - 1 < n:
                        b = (s - 1) % 3
                        k = width(l, s - 1) - (STEPS[l][s - 1][0] == "win")
                        dve.wait_ge(exp_done, g)
                        link(v.reciprocal(rsum[:, b, :], esum[:, b, :]))
                        for q in range(2):
                            ins = v.tensor_scalar(S[b][:, q, 0:k], S[b][:, q, 0:k], rsum[:, b, q:q + 1], None, ALU.mult)
                        ins.then_inc(p_ready, 1)
                    if s < n:
                        dve.wait_ge(s_act, g + 1)
                        if not on_ctx:
                            dve.wait_ge(s_dve, lat_steps(l, s))
                        v.tensor_reduce(negmax[:, s % 3, :], buf[:, :, 0:w], AX.X, ALU.max, negate=True)\
                            .then_inc(max_ready, 1)

            def gates(l):
                n = QN[l]

                def merged_lo(q):
                    dve.wait_ge(m_hi_ready, 8 * l + q + 1)
                    v.tensor_tensor(h_lo[:, q, 0:n], mT[:, q, 0:n], h_hi[:, q, 0:n].bitcast(F32), ALU.subtract)\
                        .then_inc(m_lo_ready, 1)

                for pair in range(4):
                    for g in range(3 * pair, 3 * pair + 3):
                        split_ahead(split_w, ("gate", l, g), ("gate", l, g + 1) if g < 11 else ("wo", l, 0))
                    for half in range(2):
                        for b in range(3):
                            dve.wait_ge(branch_done, 24 * l + 6 * pair + 3 * half + b + 1)
                            dve.wait_ge(sig_ready, 24 * l + 6 * pair + 2 * b + half + 1)
                            s = sig[2 * b + half][:, 0:n]
                            v.tensor_tensor(s, s, banks[:, (12 * pair + 6 + 3 * half + b) % 8, 0:n], ALU.mult)\
                                .then_inc(gated, 1)
                            if pair == 3:
                                merged_lo(3 * half + b)
                merged_lo(6)
                merged_lo(7)

            def residual(l):
                dve.wait_ge(gate_ready, l + 1)
                for c in range(4):
                    split_ahead(split_w, ("wo", l, c), ("wo", l, c + 1) if c < 3 else None)
                    for tt in range(QT[l]):
                        r = c * QT[l] + tt
                        dve.wait_ge(wo_done, 4 * QT0[l] + r + 1)
                        if r >= 4:
                            dve.wait_ge(x_attn, 4 * QT0[l] + r - 3)
                        v.tensor_tensor(upd[r % 4], banks[:, r % 8, 0:CW], gate_bc[tt // 2][:, c * CW:(c + 1) * CW],
                                        ALU.mult).then_inc(upd_ready, 1)

            def route(l):
                nt = QT[l]
                dve.wait_ge(lg_done, l + 1)
                link(v.memset(g8[:, :, :], NEG))
                link(v.tensor_tensor(lg[:, 0:nt, :], banks[:, 0, 0:nt * NR].rearrange("p (t n) -> p t n", t=nt),
                                     b_router[:, :].unsqueeze(1).to_broadcast([P, nt, NR]), ALU.add))
                link(v.tensor_copy(g8[:, 0:nt, 0:NG], lg[:, 0:nt, 0:NG]))
                for tt in range(nt):
                    ins = v.max(top_g[:, tt, :], g8[:, tt, :])
                link(ins)
                for tt in range(nt):
                    v.max_index(idx_g[:, tt, :], top_g[:, tt, :], g8[:, tt, :])
                v.tensor_tensor(prod[:, 0, 0:nt, 0:8], g8[:, 0:nt, :], top_g[:, 0:nt, 0:1].to_broadcast([P, nt, 8]),
                                ALU.subtract).then_inc(router_exp_in, 1)
                dve.wait_ge(router_exp_in, 2 * l + 1)
                link(v.tensor_copy(rt[:, 0:nt], idx_g[:, 0:nt, 0]))
                oh = cnt[:, 0:4 * nt].rearrange("p (t g) -> p t g", g=NG)
                pen = cnt[:, 16:16 + 4 * nt].rearrange("p (t g) -> p t g", g=NG)
                link(v.tensor_tensor(oh, C["iota"][:, 0:NG].unsqueeze(1).to_broadcast([P, nt, NG]),
                                     rt[:, 0:nt].unsqueeze(2).to_broadcast([P, nt, NG]), ALU.is_equal))
                link(v.tensor_scalar(pen, oh, -1.0, -NEG, ALU.add, ALU.mult))
                le4 = lem[:, 0:nt, :].rearrange("p t (g e) -> p t g e", g=NG)
                link(v.tensor_tensor(le4, lg[:, 0:nt, NG:NR].rearrange("p t (g e) -> p t g e", g=NG),
                                     oh.unsqueeze(3).to_broadcast([P, nt, NG, EPG]), ALU.mult))
                link(v.tensor_tensor(le4, le4, pen.unsqueeze(3).to_broadcast([P, nt, NG, EPG]), ALU.add))
                for tt in range(nt):
                    ins = v.max(top_e[:, tt, :], lem[:, tt, :])
                link(ins)
                for tt in range(nt):
                    ins = v.max_index(idx_e[:, tt, :], top_e[:, tt, :], lem[:, tt, :])
                link(ins)
                ef = slots_f
                link(v.tensor_copy(ef[:, :, 0:nt], idx_e[:, 0:nt, 0:2].rearrange("p t c -> p c t")))
                for c in range(2):
                    ins = v.tensor_tensor(pick[:, c, 0:nt, :], C["iota"].unsqueeze(1).to_broadcast([P, nt, NE]),
                                          ef[:, c, 0:nt].unsqueeze(2).to_broadcast([P, nt, NE]), ALU.is_equal)
                link(ins)
                v.tensor_tensor(both[:, 0:nt, :], pick[:, 0, 0:nt, :], pick[:, 1, 0:nt, :], ALU.add)\
                    .then_inc(pick_ready, 1)
                v.tensor_tensor(rt[:, 12:12 + nt], top_e[:, 0:nt, 1], top_e[:, 0:nt, 0], ALU.subtract)\
                    .then_inc(router_exp_in, 1)

            def weights(l):
                nt = QT[l]
                dve.wait_ge(router_exp, 2 * l + 2)
                link(v.tensor_reduce(rt[:, 4:4 + nt], prod[:, 0, 0:nt, 0:8], AX.X, ALU.add))
                link(v.tensor_scalar(rt[:, 20:20 + nt], rt[:, 16:16 + nt], 1.0, None, ALU.add))
                link(v.tensor_tensor(rt[:, 24:24 + nt], rt[:, 20:20 + nt], rt[:, 4:4 + nt], ALU.mult))
                link(v.reciprocal(wts[:, 0, 0:nt], rt[:, 24:24 + nt]))
                v.tensor_tensor(wts[:, 1, 0:nt], wts[:, 0, 0:nt], rt[:, 16:16 + nt], ALU.mult).then_inc(wts_ready, 1)

            def place(l):
                nt = QT[l]
                def picked(dst, table):
                    link(v.tensor_tensor(prod[:, 0, 0:nt, :], pick[:, 0, 0:nt, :], table, ALU.mult))
                    link(v.tensor_tensor(prod[:, 1, 0:nt, :], pick[:, 1, 0:nt, :], table, ALU.mult))
                    link(v.tensor_reduce(dst, prod[:, :, 0:nt, :], AX.X, ALU.add))

                def small(n):
                    return rt[:, n:n + 2 * nt].rearrange("p (c t) -> p c t", c=2)

                rr, s0, s1 = small(32), small(40), small(48)
                picked(s0, C["slot0"].unsqueeze(1).to_broadcast([P, nt, NE]))
                dve.wait_ge(rank_done, l + 1)
                v.tensor_copy(rank[:, 0:nt, :], banks[:, 1, 0:nt * NE].rearrange("p (t e) -> p t e", t=nt))
                link(v.tensor_copy(cnt[:, 0:NE], banks[:, 1, 4 * NE:5 * NE]))
                picked(rr, rank[:, 0:nt, :])
                over = prod[:, :, :, :].rearrange("p a b c -> p (a b c)")[:, 0:NE * (NBK - 1)]\
                    .rearrange("p (e m) -> p e m", e=NE)
                link(v.tensor_tensor(over, cnt[:, 0:NE].unsqueeze(2).to_broadcast([P, NE, NBK - 1]),
                                     C["thr"].unsqueeze(1).to_broadcast([P, NE, NBK - 1]), ALU.is_gt))
                nx, xin, alt = (cnt[:, q * NE:(q + 1) * NE] for q in (1, 2, 3))
                link(v.tensor_reduce(nx, over, AX.X, ALU.add))
                link(v.tensor_tensor_scan(xin, C["ones"][:, 0:NE], nx, 0.0, ALU.mult, ALU.add))
                link(v.tensor_tensor(alt, xin, nx, ALU.subtract))
                link(v.tensor_scalar(alt, alt, float(CAP), float(MAIN - CAP), ALU.mult, ALU.add))
                link(v.tensor_tensor(alt, alt, C["slot0"], ALU.subtract))
                picked(s1, alt.unsqueeze(1).to_broadcast([P, nt, NE]))
                ge = rt[:, 56:56 + 2 * nt].rearrange("p (c t) -> p c t", c=2)
                link(v.tensor_scalar(ge, rr, float(CAP), None, ALU.is_ge))
                link(v.tensor_tensor(s1, s1, ge, ALU.mult))
                link(v.tensor_tensor(s0, s0, rr, ALU.add))
                link(v.tensor_tensor(slots_f[:, :, 0:nt], s0, s1, ALU.add))
                v.tensor_copy(slots_u[:, :, 0:nt], slots_f[:, :, 0:nt]).then_inc(slots_ready, 1)
                nb = SPILL[0]
                cmp = prod[0:1, :, :, :].rearrange("p a b c -> p (a b c)")
                own = rank[0:1, :, :].rearrange("p a b -> p (a b)")
                for half in range(2):
                    hb = nb // 2
                    cc = cmp[:, 0:hb * NE].rearrange("p (b e) -> p b e", b=hb)
                    link(v.tensor_tensor(cc, xin[0:1, :].unsqueeze(1).to_broadcast([1, hb, NE]),
                                         C["iota"][0:1, half * hb:(half + 1) * hb].unsqueeze(2).to_broadcast([1, hb, NE]),
                                         ALU.is_le))
                    link(v.tensor_reduce(own[:, 1 + half * hb:1 + (half + 1) * hb], cc, AX.X, ALU.add))
                link(v.tensor_scalar(own[:, 1:1 + nb], own[:, 1:1 + nb], float(NE - 1), None, ALU.min))
                link(v.tensor_copy(own[:, 0:1], xin[0:1, NE - 1:NE]))
                v.tensor_copy(meta[:, :], own[:, 0:1 + nb]).then_inc(meta_ready, 1)

            def take_xT(l, e, i=None):
                n = E0[l] + e
                if n >= 3:
                    dve.wait_ge(e_up_done, lin(i, n - 2, UNROLL))
                dve.wait_ge(xe_turned, lin(i, n + 1, UNROLL))
                v.tensor_copy(xeT[n % 3], banks[:, 0, :].rearrange("p (k s) -> p k s", k=KD)).then_inc(xeT_ready, 1)

            def take_hid(l, e, i=None):
                n = E0[l] + e
                if n:
                    dve.wait_ge(hid_turned, lin(i, n, UNROLL))
                dve.wait_ge(silu_ready, lin(i, n + 1, UNROLL))
                dve.wait_ge(e_up_done, lin(i, n + 1, UNROLL))
                v.tensor_tensor(hid, act_g, banks[0:CAP, 3, 0:DE], ALU.mult).then_inc(hid_ready, 1)

            def take_hidT(l, e, i=None):
                n = E0[l] + e
                if n:
                    dve.wait_ge(down_done, lin(i, n, UNROLL))
                dve.wait_ge(hid_turned, lin(i, n + 1, UNROLL))
                v.tensor_copy(hidT[:, :, :], banks[:, 1, 0:2 * CAP].rearrange("p (k s) -> p k s", k=2))\
                    .then_inc(hidT_ready, 1)

            def expert_step(l, e, i=None):
                take_hidT(l, e, i)
                if e + 2 < NE:
                    take_xT(l, e + 2, i)
                if e + 1 < NE:
                    take_hid(l, e + 1, i)

            def experts(l):
                take_xT(l, 0)
                take_xT(l, 1)
                take_hid(l, 0)
                for e in range(3):
                    expert_step(l, e)
                with dve.Fori(0, LOOPED) as i:
                    for e in range(3, 3 + UNROLL):
                        expert_step(l, e, i)
                for e in range(NE - 5, NE):
                    expert_step(l, e)

            def spill(l):
                n_spill = dve.value_load(meta[0:1, 0:1], min_val=0, max_val=SPILL[l])
                step = spill_step[l]
                with dve.If(n_spill > 0):
                    with dve.Fori(0, SPILL[l]) as b:
                        with dve.If(b < n_spill):
                            dve.wait_ge(step, b * 9 + 2)
                            v.tensor_copy(xeT[0], banks[:, 0, :].rearrange("p (k s) -> p k s", k=KD)).then_inc(step, 1)
                            dve.wait_ge(step, b * 9 + 5)
                            v.tensor_tensor(hid, act_g, banks[0:CAP, 3, 0:DE], ALU.mult).then_inc(step, 1)
                            dve.wait_ge(step, b * 9 + 7)
                            v.tensor_copy(hidT[:, :, :], banks[:, 1, 0:2 * CAP].rearrange("p (k s) -> p k s", k=2))\
                                .then_inc(step, 1)

            def combine(l):
                between = [(14, 17), (17, 18), (18, 20), ()] if l == 0 else [()] * 2
                dve.wait_ge(gate_f_ready, l + 1)
                dve.wait_ge(wts_ready, l + 1)
                for tt in range(QT[l]):
                    for c in range(*between[tt]) if between[tt] else ():
                        mod_add(1, c)
                    y0, y1 = got[tt]
                    dve.wait_ge(y_weighted, QT0[l] + tt + 1)
                    link(v.scalar_tensor_tensor(y0, y0, wts[:, 0, tt:tt + 1], y1, ALU.mult, ALU.add))
                    v.tensor_tensor(y0, y0, gate_f[tt // 2], ALU.mult).then_inc(y_gated, 1)

            for l in range(DEPTH):
                if l == 0:
                    for c in range(8):
                        mod_add(0, c)
                    rstd(0, NORM_TILES[0])
                    scales(0)
                    for c in range(8, 12):
                        mod_add(0, c)
                norm(2 * l)
                project(l)
                attention(l)
                gates(l)
                residual(l)
                if l == 0:
                    rstd(1, NORM_TILES[1])
                    for c in range(12, 20):
                        mod_add(0, c)
                    scales(1)
                else:
                    scales(3)
                    rstd(3, NORM_TILES[3])
                norm(2 * l + 1)
                route(l)
                if l == 0:
                    for c in range(20, 24):
                        mod_add(0, c)
                weights(l)
                place(l)
                if l == 0:
                    for c in range(12):
                        mod_add(1, c)
                experts(l)
                if l == 0:
                    for c in (12, 13):
                        mod_add(1, c)
                spill(l)
                combine(l)
                if l == 0:
                    for c in range(20, 24):
                        mod_add(1, c)
                    scales(2)
                    rstd(2, NORM_TILES[2])

            rstd(4, [0, 1])
            dve.wait_ge(g_in, 80)
            for tt in range(2):
                v.scalar_tensor_tensor(htok[:, tt, :], X[:, tt, :], stat[:, 12 + tt:13 + tt], g_bc,
                                       ALU.mult, ALU.mult).then_inc(fin_ready, 1)


INPUTS = ["x", "c", "ctx", "c_ctx", "w_mod", "b_mod", "g_attn", "g_ffn", "w_in", "conv_w", "rpb", "sinks",
          "w_branch", "w_o", "w_rg", "b_rg", "w_re", "b_re", "w_e_gate", "w_e_up", "w_e_down", "g_final"]


def kernel(**inputs):
    import concourse.bacc as bacc
    from concourse.bass_utils import run_bass_kernel_spmd

    nc = bacc.Bacc("TRN2", target_bir_lowering=False, num_devices=1)
    arrays, t = {}, {}
    given = {n: np.ascontiguousarray(inputs[n]) for n in INPUTS}
    given["conv_w"] = np.ascontiguousarray(given["conv_w"].transpose(0, 2, 1))
    given["consts"] = constants()
    for name, a in given.items():
        arrays[f"in_{name}"] = a
        t[name] = nc.dram_tensor(f"in_{name}", a.shape, mybir.dt.from_np(a.dtype), kind="ExternalInput").ap()
    out = nc.dram_tensor("out", (1, SEQ, D), F32, kind="ExternalOutput").ap()
    program(nc, t, out)
    return run_bass_kernel_spmd(nc, [arrays], core_ids=[0]).results[0]["out"]
```
